# Optimizing a Trainium2 kernel written in Bass

```python
import math
import jax, jax.numpy as jnp
from jax import lax
import numpy as np

D_MODEL = 1024
BATCH = 1
SEQ = 256
DEPTH = 1

CONV_MIX_WIDTH = 1024
SHORT_CONV_WIDTH = 3
N_HEADS = 8
HEAD_DIM = 128
ATTN_WIDTH = N_HEADS * HEAD_DIM
MOBA_BLOCK = 256
MOBA_TOP_K = 3
Q_CHUNK = 32
ROPE_THETA = 10000.0
D_FF = 2816
FFN_CONV_WIDTH = 3

RMS_EPS = 1e-6
NEG_INF = -1e30
PROJ_WIDTH = 3 * CONV_MIX_WIDTH + 3 * ATTN_WIDTH + 2 * D_MODEL

kernel_name = "hybrid_gated_conv_moba_convffn"

def rmsnorm(x, g):
    xf = x.astype(jnp.float32)
    y = xf * lax.rsqrt(jnp.mean(xf * xf, axis=-1, keepdims=True) + RMS_EPS)
    return (y * g.astype(jnp.float32)).astype(x.dtype)

def causal_dwconv(x, w):
    width = w.shape[0]
    s = x.shape[1]
    xp = jnp.pad(x, ((0, 0), (width - 1, 0), (0, 0)))
    return sum(xp[:, i:i + s, :] * w[i] for i in range(width))

def rope(x, positions):
    hd = x.shape[-1]
    half = hd // 2
    inv_freq = jnp.exp(-math.log(ROPE_THETA) * jnp.arange(half, dtype=jnp.float32) * (2.0 / hd))
    ang = positions.astype(jnp.float32)[:, None, :, None] * inv_freq
    cos, sin = jnp.cos(ang), jnp.sin(ang)
    xf = x.astype(jnp.float32)
    x1, x2 = xf[..., :half], xf[..., half:]
    out = jnp.concatenate([x1 * cos - x2 * sin, x2 * cos + x1 * sin], axis=-1)
    return out.astype(x.dtype)

def moba_attention(q, k, v):
    b, h, s, hd = q.shape
    n_blk = -(-s // MOBA_BLOCK)
    s_pad = n_blk * MOBA_BLOCK
    pad = ((0, 0), (0, 0), (0, s_pad - s), (0, 0))
    q, k, v = jnp.pad(q, pad), jnp.pad(k, pad), jnp.pad(v, pad)
    kb = k.reshape(b, h, n_blk, MOBA_BLOCK, hd)
    vb = v.reshape(b, h, n_blk, MOBA_BLOCK, hd)

    k_mean = jnp.mean(kb.astype(jnp.float32), axis=3)
    gate = jnp.einsum('bhsd,bhnd->bhsn', q.astype(jnp.float32), k_mean)
    q_blk_all = jnp.arange(s_pad) // MOBA_BLOCK
    past = jnp.arange(n_blk)[None, :] < q_blk_all[:, None]
    gate = jnp.where(past, gate, NEG_INF)
    k_sel = min(MOBA_TOP_K, n_blk)
    _, sel = lax.top_k(gate, k_sel)

    scale = hd ** -0.5
    b_ix = jnp.arange(b)[:, None, None, None]
    h_ix = jnp.arange(h)[None, :, None, None]

    def chunk(c):
        start = c * Q_CHUNK
        q_c = lax.dynamic_slice_in_dim(q, start, Q_CHUNK, axis=2)
        sel_c = lax.dynamic_slice_in_dim(sel, start, Q_CHUNK, axis=2)
        q_pos = start + jnp.arange(Q_CHUNK)
        blk_start = (start // MOBA_BLOCK) * MOBA_BLOCK
        k_g = kb[b_ix, h_ix, sel_c]
        v_g = vb[b_ix, h_ix, sel_c]
        s_sel = jnp.einsum('bhqd,bhqjkd->bhqjk', q_c, k_g,
                           preferred_element_type=jnp.float32) * scale
        valid = sel_c < (q_pos // MOBA_BLOCK)[None, None, :, None]
        s_sel = jnp.where(valid[..., None], s_sel, NEG_INF).reshape(b, h, Q_CHUNK, k_sel * MOBA_BLOCK)
        k_own = lax.dynamic_slice_in_dim(k, blk_start, MOBA_BLOCK, axis=2)
        v_own = lax.dynamic_slice_in_dim(v, blk_start, MOBA_BLOCK, axis=2)
        s_own = jnp.einsum('bhqd,bhkd->bhqk', q_c, k_own,
                           preferred_element_type=jnp.float32) * scale
        causal = (blk_start + jnp.arange(MOBA_BLOCK))[None, :] <= q_pos[:, None]
        s_own = jnp.where(causal, s_own, NEG_INF)
        p = jax.nn.softmax(jnp.concatenate([s_sel, s_own], axis=-1), axis=-1).astype(v.dtype)
        p_sel = p[..., :k_sel * MOBA_BLOCK].reshape(b, h, Q_CHUNK, k_sel, MOBA_BLOCK)
        p_own = p[..., k_sel * MOBA_BLOCK:]
        return (jnp.einsum('bhqjk,bhqjkd->bhqd', p_sel, v_g)
                + jnp.einsum('bhqk,bhkd->bhqd', p_own, v_own))

    out = lax.map(chunk, jnp.arange(s_pad // Q_CHUNK))
    out = out.transpose(1, 0, 3, 2, 4).reshape(b, s_pad, h, hd)[:, :s]
    return out.reshape(b, s, h * hd)

def hybrid_mixer(xn, positions, w_in, conv_w, w_conv_out, w_attn_out, w_out):
    b, s, _ = xn.shape
    proj = xn @ w_in
    cuts = np.cumsum([CONV_MIX_WIDTH] * 3 + [ATTN_WIDTH] * 3 + [D_MODEL])
    c_b, c_c, c_x, q, k, v, g_conv, g_attn = jnp.split(proj, [int(i) for i in cuts], axis=-1)
    y_conv = (c_b * causal_dwconv(c_c * c_x, conv_w)) @ w_conv_out
    to_heads = lambda t: t.reshape(b, s, N_HEADS, HEAD_DIM).transpose(0, 2, 1, 3)
    q = rope(to_heads(q), positions)
    k = rope(to_heads(k), positions)
    y_attn = moba_attention(q, k, to_heads(v)) @ w_attn_out
    merged = jax.nn.sigmoid(g_conv) * y_conv + jax.nn.sigmoid(g_attn) * y_attn
    return merged @ w_out

def conv_gated_mlp(xn, w_ffn_in, ffn_conv_w, ffn_conv_b, w_ffn_down):
    u, g = jnp.split(xn @ w_ffn_in, 2, axis=-1)
    g = causal_dwconv(g, ffn_conv_w) + ffn_conv_b
    return (jax.nn.silu(g) * u) @ w_ffn_down

def setup_inputs(seed: int = 0) -> dict:
    key = jax.random.key(seed)
    ks = jax.random.split(key, 16)
    f32 = jnp.float32

    def dense(k, fan_in, shape):
        return jax.random.normal(k, shape, f32) * fan_in ** -0.5

    def gain(k, shape):
        return 1.0 + 0.05 * jax.random.normal(k, shape, f32)

    x = jax.random.normal(ks[0], (BATCH, SEQ, D_MODEL), f32)
    positions = jnp.broadcast_to(jnp.arange(SEQ, dtype=jnp.int32)[None, :], (BATCH, SEQ))
    return {
        "x": x,
        "positions": positions,
        "norm_mix_g": gain(ks[1], (DEPTH, D_MODEL)),
        "w_in": dense(ks[2], D_MODEL, (DEPTH, D_MODEL, PROJ_WIDTH)),
        "conv_w": dense(ks[3], SHORT_CONV_WIDTH, (DEPTH, SHORT_CONV_WIDTH, CONV_MIX_WIDTH)),
        "w_conv_out": dense(ks[4], CONV_MIX_WIDTH, (DEPTH, CONV_MIX_WIDTH, D_MODEL)),
        "w_attn_out": dense(ks[5], ATTN_WIDTH, (DEPTH, ATTN_WIDTH, D_MODEL)),
        "w_out": dense(ks[6], D_MODEL, (DEPTH, D_MODEL, D_MODEL)),
        "norm_ffn_g": gain(ks[7], (DEPTH, D_MODEL)),
        "w_ffn_in": dense(ks[8], D_MODEL, (DEPTH, D_MODEL, 2 * D_FF)),
        "ffn_conv_w": dense(ks[9], FFN_CONV_WIDTH, (DEPTH, FFN_CONV_WIDTH, D_FF)),
        "ffn_conv_b": 0.02 * jax.random.normal(ks[10], (DEPTH, D_FF), f32),
        "w_ffn_down": dense(ks[11], D_FF, (DEPTH, D_FF, D_MODEL)),
        "norm_final_g": gain(ks[12], (D_MODEL,)),
    }

def reference(x, positions, norm_mix_g, w_in, conv_w, w_conv_out, w_attn_out, w_out,
              norm_ffn_g, w_ffn_in, ffn_conv_w, ffn_conv_b, w_ffn_down, norm_final_g):
    h = x
    for layer in range(DEPTH):
        xn = rmsnorm(h, norm_mix_g[layer])
        h = h + hybrid_mixer(xn, positions, w_in[layer], conv_w[layer], w_conv_out[layer],
                             w_attn_out[layer], w_out[layer])
        xn = rmsnorm(h, norm_ffn_g[layer])
        h = h + conv_gated_mlp(xn, w_ffn_in[layer], ffn_conv_w[layer], ffn_conv_b[layer],
                               w_ffn_down[layer])
    return rmsnorm(h, norm_final_g)


_drawn_inputs = setup_inputs


def setup_inputs(seed=0):
    import zlib

    import numpy as np

    out = dict(_drawn_inputs(seed))
    spreads = {}
    factors = {'ffn_conv_b': 6.17}
    for name, (base, spread) in spreads.items():
        noise = np.random.default_rng([zlib.crc32(name.encode()), seed]).standard_normal(out[name].shape)
        drawn = base * np.exp(spread * noise) if base else spread * noise
        out[name] = __import__('jax').numpy.asarray(drawn.astype(out[name].dtype))
    for name, factor in factors.items():
        out[name] = (out[name] * factor).astype(out[name].dtype)
    return out
```

```python
import math
from contextlib import ExitStack

import numpy as np
import concourse.bass as bass
from concourse import mybir

F32 = mybir.dt.float32
F32R = mybir.dt.float32r
I32 = mybir.dt.int32
ALU = mybir.AluOpType
ACT = mybir.ActivationFunctionType

P = 128
D = 1024
S = 256
TT = S // P
KD = D // P
HD = 128
DFF = 2816
NF = DFF // P
NP = NF // 2
BLK = 2048
COLS = BLK // KD
EPS = 1e-6
SCALE = HD ** -0.5
NEG = -1e30
RING = 4
RING_F = 3
BANKS = 4
STEPS = 4
PER_STEP = 8
N_D = STEPS * PER_STEP
N_E = N_D + 8
N_F = N_E + 4
USES_F = 2 * N_F // BANKS

X, C, Q, K, V, B, GC, GA = range(PER_STEP)
W_IN_PART = {X: 2, C: 1, Q: 3, K: 4, V: 5, B: 0, GC: 6, GA: 7}

ROW_CONV = 0
ROW_FCONV = ROW_CONV + 3 * KD
ROW_FBIAS = ROW_FCONV + 3 * NF
ROW_GMIX = ROW_FBIAS + NF
ROW_GFFN = ROW_GMIX + KD
assert ROW_GFFN + KD == P

ROUND = 1.5 * 2.0 ** 23
PI_IN = 3.1415925
ANGLE_STEPS = 22


def cut(value, bits, parts):
    out = []
    for _ in range(parts):
        e = math.floor(math.log2(abs(value))) - bits + 1
        out.append(math.floor(value / 2.0 ** e) * 2.0 ** e)
        value -= out[-1]
    return out + [float(np.float32(value))]


def layer(nc, x, positions, norm_mix_g, w_in, conv_w, w_conv_out, w_attn_out, w_out, norm_ffn_g,
          w_ffn_in, ffn_conv_w, ffn_conv_b, w_ffn_down, norm_final_g, rope_cols, out):
    rows = lambda w: w[0].rearrange("(k p) n -> p k n", p=P)
    w_in_v, w_conv_out_v, w_attn_out_v, w_out_v, w_ffn_in_v, w_ffn_down_v = map(
        rows, (w_in, w_conv_out, w_attn_out, w_out, w_ffn_in, w_ffn_down))
    x_v = x[0].rearrange("(t p) d -> p t d", p=P)
    out_v = out[0].rearrange("(t p) d -> p t d", p=P)

    ctx = ExitStack()
    with ctx:
        sb = lambda name, shape, dt=F32: ctx.enter_context(nc.sbuf_tensor(name, shape, dt))
        sem = lambda name: ctx.enter_context(nc.semaphore(name))

        raw = [sb(f"raw{i}", [P, BLK]) for i in range(RING)]
        w_hi = [sb(f"w_hi{i}", [P, BLK], F32R) for i in range(RING)]
        w_lo = [sb(f"w_lo{i}", [P, BLK], F32R) for i in range(RING)]
        xm_hi, xm_lo = sb("xm_hi", [P, KD, S], F32R), sb("xm_lo", [P, KD, S], F32R)
        zh_hi, zh_lo = sb("zh_hi", [P, KD, S], F32R), sb("zh_lo", [P, KD, S], F32R)
        attn_hi, attn_lo = sb("attn_hi", [P, KD, S], F32R), sb("attn_lo", [P, KD, S], F32R)
        ffn_hi, ffn_lo = attn_hi, attn_lo
        x_tok = sb("x_tok", [P, TT, D])
        scratch = sb("scratch", [P, TT, D])
        xn_tok = scratch
        gate_c, gate_a = sb("gate_c", [P, KD, S]), sb("gate_a", [P, KD, S])
        hT = gate_c
        consts_rows = sb("consts_rows", [P, P])
        consts = sb("consts", [P, P])
        ident, ones = sb("ident", [P, P]), sb("ones", [P, P])
        mask = sb("mask", [P, 3 * P])
        cosT, sinT = sb("cosT", [P, S]), sb("sinT", [P, S])
        rope_c = sb("rope_c", [P, 3])
        xs = sb("xs", [P, 2, S])
        cx = sb("cx", [P, 2, S + 2])
        conv = sb("conv", [P, 2, S])
        z = conv
        rope_a, rope_b = sb("rope_a", [P, 4, S]), sb("rope_b", [P, 4, S])
        qkT = sb("qkT", [P, 4, S])
        v_tok = sb("v_tok", [P, TT, 2 * HD])
        flat = scratch[:, :, :].rearrange("p t d -> p (t d)")
        masked = flat[:, 0:6 * P].rearrange("p (h s) -> p h s", h=2)
        probs = flat[:, 6 * P:12 * P].rearrange("p (h s) -> p h s", h=2)
        probs_n = masked
        probsT = sb("probsT", [P, 2, 3 * P])
        row_max, neg_max = sb("row_max", [P, 4]), sb("neg_max", [P, 4])
        row_sum, row_inv = sb("row_sum", [P, 4]), sb("row_inv", [P, 4])
        gated_c, gated_a = rope_a, rope_b
        merged = qkT
        up, silu = rope_a, rope_b
        fg = sb("fg", [P, 2, S + 2])
        fconv = qkT
        act = z
        sumsq = xs
        spare = gate_a[:, :, :].rearrange("p j s -> p (j s)")
        g_final = spare[:, 0:D]
        diag = spare[:, D:D + S].rearrange("p (t s) -> p t s", t=TT)
        rstd_b = spare[:, D + S:D + 2 * S]
        sums = sb("sums", [P, 8])
        means = sb("means", [P, 8])
        rstd = sb("rstd", [P, 8])
        minus_half = sb("minus_half", [P, 2])
        pos_i = rope_a[:, 0, :].bitcast(I32)
        angle = gate_a

        ring_ps = [ctx.enter_context(nc.psum_tensor(f"ring_ps{i}", [P, 2 * S], F32))[:, 0:S]
                   for i in range(BANKS)]
        wide = ctx.enter_context(nc.psum_tensor("wide", [P, 4, 512], F32))

        x_loaded = [sem(f"x_loaded{t}") for t in range(TT)]
        rows_loaded = sem("rows_loaded")
        rope_loaded = sem("rope_loaded")
        g_final_loaded = sem("g_final_loaded")
        raw_loaded = [sem(f"raw_loaded{i}") for i in range(RING)]
        hi_ready = sem("hi_ready")
        lo_ready = sem("lo_ready")
        slots_seen = sem("slots_seen")
        left_done = sem("left_done")
        block_done = sem("block_done")
        evacuated = [sem(f"evacuated{i}") for i in range(BANKS)]
        setup = sem("setup")
        pool_steps = sem("pool_steps")
        sums_ready = sem("sums_ready")
        means_ready = sem("means_ready")
        rstd_ready = sem("rstd_ready")
        xn_ready = sem("xn_ready")
        consts_seen = sem("consts_seen")
        consts_ready = sem("consts_ready")
        xT_done = sem("xT_done")
        x_hi_ready, x_lo_ready = sem("x_hi_ready"), sem("x_lo_ready")
        angles = sem("angles")
        tables_ready = sem("tables_ready")
        taps = sem("taps")
        z_hi_ready, z_lo_ready = sem("z_hi_ready"), sem("z_lo_ready")
        rope_added = sem("rope_added")
        scores_done, masked_done = sem("scores_done"), sem("masked_done")
        neg_max_ready, exp_done = sem("neg_max_ready"), sem("exp_done")
        inv_ready, probs_ready = sem("inv_ready"), sem("probs_ready")
        probsT_done, probsT_ready = sem("probsT_done"), sem("probsT_ready")
        attn_done = sem("attn_done")
        attn_hi_ready, attn_lo_ready = sem("attn_hi_ready"), sem("attn_lo_ready")
        merged_ready = sem("merged_ready")
        m_hi_ready, m_lo_ready = sem("m_hi_ready"), sem("m_lo_ready")
        squares_ready, sumsq_ready = sem("squares_ready"), sem("sumsq_ready")
        h_hi_ready = sem("h_hi_ready")
        stats_done, diag_ready, bcast_done = sem("stats_done"), sem("diag_ready"), sem("bcast_done")
        rstd_b_ready = sem("rstd_b_ready")
        ftap, ftaps_dve = sem("ftap"), sem("ftaps_dve")
        silu_ready, act_ready = sem("silu_ready"), sem("act_ready")
        a_hi_ready, a_lo_ready = sem("a_hi_ready"), sem("a_lo_ready")
        final_done = sem("final_done")
        out_ready, out_stored = sem("out_ready"), sem("out_stored")

        left = lambda n: n + 1
        done = lambda n: n + 1 + RING
        slot_free = lambda n: done(n - RING)
        free_for = lambda k: k + 1
        read_out = lambda k: k + 2

        block = ctx.enter_context(nc.Block())

        @block.sync
        def _(sp):
            def load(slot, use, n, source):
                if n is not None:
                    sp.wait_ge(lo_ready, n - RING + 1)
                    sp.sem_inc(slots_seen, 1)
                sp.dma_start(raw[slot][:, :].rearrange("p (k c) -> p k c", k=source.shape[1]),
                             source).then_inc(raw_loaded[slot], 16)

            part = lambda b, c: w_in_v[:, :, bass.ds(W_IN_PART[b] * D + COLS * c, COLS)]
            for t in range(TT):
                sp.dma_start(x_tok[:, t, :], x_v[:, t, :]).then_inc(x_loaded[t], 16)
            for b in range(RING):
                load(b, 0, None, part(b, 0))
            with sp.Fori(0, STEPS - 1) as c:
                for b in range(RING, PER_STEP):
                    load(b % RING, None, PER_STEP * c + b, part(b, c))
                for b in range(RING):
                    load(b, None, PER_STEP * c + b + PER_STEP, part(b, c + 1))
            for b in range(RING, PER_STEP):
                load(b % RING, None, PER_STEP * (STEPS - 1) + b, part(b, STEPS - 1))
            for j in range(4):
                for i, source in enumerate((w_conv_out_v, w_attn_out_v)):
                    n = N_D + 2 * j + i
                    load(n % RING, None, n, source[:, :, COLS * j:COLS * (j + 1)])
            for j in range(4):
                load(j, None, N_E + j, w_out_v[:, :, COLS * j:COLS * (j + 1)])

            def load_f(m, n_split, source):
                sp.wait_ge(lo_ready, n_split)
                sp.sem_inc(slots_seen, 1)
                sp.dma_start(raw[m][:, :].rearrange("p (k c) -> p k c", k=source.shape[1]),
                             source).then_inc(raw_loaded[m], 16)

            up_cols = lambda p: w_ffn_in_v[:, :, bass.ds(COLS * p, COLS)]
            gate_cols = lambda p: w_ffn_in_v[:, :, bass.ds(DFF + COLS * p, COLS)]
            down_rows = lambda p: w_ffn_down_v[:, bass.ds(2 * p, 2), :]
            load_f(0, N_F - 3, up_cols(0))
            load_f(1, N_F - 2, gate_cols(0))
            load_f(2, N_F - 1, up_cols(1))
            load_f(0, N_F + 1, gate_cols(1))
            load_f(1, N_F + 2, down_rows(0))
            with sp.Fori(2, NP) as p:
                load_f(2, N_F + 3 * p - 3, up_cols(p))
                load_f(0, N_F + 3 * p - 2, gate_cols(p))
                load_f(1, N_F + 3 * p - 1, down_rows(p - 1))
            load_f(2, N_F + 3 * NP - 3, down_rows(NP - 1))

            for i in range(2 * TT):
                t, half = divmod(i, 2)
                sp.wait_ge(out_ready, i + 1)
                sp.dma_start(out_v[:, t, 512 * half:512 * (half + 1)],
                             scratch[:, t, 512 * half:512 * (half + 1)]).then_inc(out_stored, 16)
            sp.wait_ge(out_stored, 16 * 2 * TT)

        @block.gpsimd
        def _(pool):
            pool.memset(ident[:, :], 0.0).then_inc(setup, 1)
            pool.memset(mask[:, :], 0.0).then_inc(setup, 1)
            pool.memset(minus_half[:, :], -0.5).then_inc(setup, 1)
            pool.wait_ge(setup, 3)
            pool.affine_select(out=ident[:, :], in_=ident[:, :], compare_op=ALU.not_equal, fill=1.0,
                               base=0, pattern=[[-1, P]], channel_multiplier=1).then_inc(setup, 1)
            for tile, at in enumerate((slice(0, P), slice(P, 3 * P))):
                pool.affine_select(out=mask[:, at], in_=mask[:, at], compare_op=ALU.is_ge, fill=NEG,
                                   base=P * tile, pattern=[[-1, P * (tile + 1)]],
                                   channel_multiplier=1).then_inc(setup, 1)
            pool.memset(ones[:, :], 1.0).then_inc(setup, 1)
            pool.memset(cx[:, :, 0:2], 0.0).then_inc(setup, 1)
            pool.memset(fg[:, :, 0:2], 0.0).then_inc(setup, 1)

            def inverse_root(at):
                pool.tensor_tensor(rstd[:, at:at + 2], means[:, at:at + 2], minus_half[:, :],
                                   ALU.pow).then_inc(rstd_ready, 1)

            pool.wait_ge(means_ready, 1)
            inverse_root(0)

            with pool.Fori(0, STEPS) as c:
                for r in range(4):
                    bank, use = r % BANKS, 4 * c + 1
                    pool.wait_ge(evacuated[bank], read_out(use))
                    pool.tensor_tensor(qkT[:, r, :], rope_a[:, r, :], rope_b[:, r, :],
                                       ALU.add).then_inc(rope_added, 1)

            with pool.Fori(0, 2) as i:
                for u in range(2):
                    for g in range(2):
                        pool.wait_ge(evacuated[2 + g], read_out(2 * N_D // BANKS + 2 * i + u))
                        pool.tensor_tensor(merged[:, 2 * u + g, :], gated_c[:, 2 * u + g, :],
                                           gated_a[:, 2 * u + g, :], ALU.add).then_inc(merged_ready, 1)

            pool.wait_ge(m_lo_ready, KD)
            pool.dma_start(g_final[:, :], norm_final_g.rearrange("(a n) -> a n", a=1)
                           .to_broadcast([P, D])).then_inc(g_final_loaded, 16)

            squares = scratch[:, :, :].rearrange("p t (j s) -> p (t j) s", s=S)
            for j in range(1, KD):
                pool.wait_ge(squares_ready, j + 1)
                if j > 1:
                    pool.wait_ge(sumsq_ready, j - 1)
                before = squares[:, 0, :] if j == 1 else sumsq[:, j % 2, :]
                pool.tensor_tensor(sumsq[:, (j + 1) % 2, :], before, squares[:, j, :],
                                   ALU.add).then_inc(sumsq_ready, 1)
            pool.wait_ge(means_ready, 2)
            inverse_root(2)

            def times_up(p, par):
                for g in range(2):
                    pool.wait_ge(silu_ready, 2 * p + g + 1)
                    pool.tensor_tensor(act[:, g, :], silu[:, 2 * par + g, :], up[:, 2 * par + g, :],
                                       ALU.mult).then_inc(act_ready, 1)

            times_up(0, 0)
            with pool.Fori(0, NP // 2) as i:
                times_up(2 * i + 1, 1)
                times_up(2 * i + 2, 0)
            for t in range(TT):
                pool.wait_ge(means_ready, 3 + t)
                pool.tensor_tensor(rstd[:, 4 + t:5 + t], means[:, 4 + t:5 + t], minus_half[:, 0:1],
                                   ALU.pow).then_inc(rstd_ready, 1)

        @block.scalar
        def _(act_):
            copy = lambda out_, in_, **k: act_.activation(out_, in_, ACT.Copy, **k)

            def split_hi(slot, use, n, free):
                act_.wait_ge(raw_loaded[slot], 16 * (use + 1))
                act_.wait_ge(block_done, free)
                copy(w_hi[slot][:, :], raw[slot][:, :]).then_inc(hi_ready, 1)

            act_.dma_start(consts_rows[ROW_CONV:ROW_FCONV, :],
                           conv_w[0].rearrange("i (j p) -> (i j) p", p=P)).then_inc(rows_loaded, 16)
            act_.dma_start(consts_rows[ROW_FCONV:ROW_FBIAS, :],
                           ffn_conv_w[0].rearrange("i (j p) -> (i j) p", p=P)).then_inc(rows_loaded, 16)
            act_.dma_start(consts_rows[ROW_FBIAS:ROW_GMIX, :],
                           ffn_conv_b[0].rearrange("(j p) -> j p", p=P)).then_inc(rows_loaded, 16)
            act_.dma_start(consts_rows[ROW_GMIX:ROW_GFFN, :],
                           norm_mix_g[0].rearrange("(j p) -> j p", p=P)).then_inc(rows_loaded, 16)
            act_.dma_start(consts_rows[ROW_GFFN:P, :],
                           norm_ffn_g[0].rearrange("(j p) -> j p", p=P)).then_inc(rows_loaded, 16)
            act_.dma_start(pos_i[:, :], positions.to_broadcast([P, S])).then_inc(rope_loaded, 16)
            act_.dma_start(rope_c[:, :], rope_cols).then_inc(rope_loaded, 16)

            for t in range(TT):
                act_.wait_ge(x_loaded[t], 16)
                act_.activation(xn_tok[:, t, :], x_tok[:, t, :], ACT.Square,
                                accum_out=sums[:, t:t + 1]).then_inc(sums_ready, 1)
            act_.wait_ge(sums_ready, TT)
            copy(means[:, 0:2], sums[:, 0:2], scale=1.0 / D, bias=EPS).then_inc(means_ready, 1)
            split_hi(0, 0, 0, slot_free(0))
            act_.wait_ge(rstd_ready, 1)
            for t in range(TT):
                copy(xn_tok[:, t, :], x_tok[:, t, :], scale=rstd[:, t:t + 1]).then_inc(xn_ready, 1)
            act_.wait_ge(consts_ready, 1)
            act_.wait_ge(xT_done, 1)
            for k in range(KD):
                copy(xm_hi[:, k, :], wide[:, k // 2, S * (k % 2):S * (k % 2 + 1)],
                     scale=consts[:, ROW_GMIX + k:ROW_GMIX + k + 1]).then_inc(x_hi_ready, 1)
            split_hi(1, 0, 1, slot_free(1))
            act_.wait_ge(angles, ANGLE_STEPS)
            act_.activation(sinT[:, :], angle[:, 4, :], ACT.Sin,
                            scale=rope_c[:, 1:2]).then_inc(tables_ready, 1)
            act_.activation(cosT[:, :], angle[:, 5, :], ACT.Sin, scale=-1.0,
                            bias=rope_c[:, 2:3]).then_inc(tables_ready, 1)

            with act_.Fori(0, STEPS) as c:
                n0 = PER_STEP * c
                for b in range(PER_STEP):
                    ahead = b + 2
                    split_hi(ahead % RING, 2 * c + ahead // RING, n0 + ahead, slot_free(n0 + ahead))
                    for g in range(2):
                        bank = (2 * b + g) % BANKS
                        if b in (X, V, GC, GA):
                            act_.wait_ge(*((left_done, left(n0 + b)) if g == 0
                                           else (block_done, done(n0 + b))))
                        if b == X:
                            copy(xs[:, g, :], ring_ps[bank][:, :]).then_inc(evacuated[bank], 1)
                        if b == V:
                            copy(v_tok[:, g, :], ring_ps[bank][:, :]).then_inc(evacuated[bank], 1)
                        if b in (GC, GA):
                            gate = gate_c if b == GC else gate_a
                            act_.activation(gate[:, bass.ds(2 * c + g, 1), :], ring_ps[bank][:, :],
                                            ACT.Tanh, scale=0.5).then_inc(evacuated[bank], 1)
                    if b == B:
                        for h in range(2):
                            act_.wait_ge(neg_max_ready, c + 1)
                            for i, at in enumerate((slice(0, P), slice(P, 3 * P))):
                                col = 2 * h + i
                                act_.activation(probs[:, h, at], masked[:, h, at], ACT.Exp,
                                                bias=neg_max[:, col:col + 1], scale=SCALE,
                                                accum_out=row_sum[:, col:col + 1]).then_inc(exp_done, 1)
                        for g in range(2):
                            bank = (2 * b + g) % BANKS
                            act_.wait_ge(evacuated[bank], read_out(4 * c + (2 * b + g) // BANKS))
                            copy(zh_hi[:, bass.ds(2 * c + g, 1), :], z[:, g, :]).then_inc(z_hi_ready, 1)
                    if b == GA:
                        for h in range(2):
                            act_.wait_ge(probsT_done, 2 * c + h + 1)
                            copy(probsT[:, h, :], wide[:, 2 + h, 0:3 * P]).then_inc(probsT_ready, 1)
                        act_.wait_ge(attn_done, c + 1)
                        copy(attn_hi[:, bass.ds(2 * c, 2), :], wide[:, 0, :]).then_inc(attn_hi_ready, 1)

            with act_.Fori(0, 2) as i:
                for q in range(4):
                    ahead = q + 2
                    n = N_D + 4 * i + ahead
                    split_hi(ahead % RING, N_D // RING + i + ahead // RING, n, slot_free(n))
                    if q % 2:
                        for g in range(2):
                            j = 4 * i + q - 1 + g
                            act_.wait_ge(merged_ready, j + 1)
                            copy(xm_hi[:, bass.ds(j, 1), :], merged[:, q - 1 + g, :],
                                 scale=0.5).then_inc(m_hi_ready, 1)
            squares = scratch[:, :, :].rearrange("p t (j s) -> p (t j) s", s=S)
            for q in range(4):
                n = N_E + q + 2
                if q < 2:
                    split_hi((q + 2) % RING, N_E // RING, n, slot_free(n))
                else:
                    split_hi(q - 2, N_F // RING, n, slot_free(n))
                for g in range(2):
                    j = 2 * q + g
                    bank = j % BANKS
                    act_.wait_ge(*((left_done, left(N_E + q)) if g == 0 else (block_done, done(N_E + q))))
                    copy(hT[:, j, :], ring_ps[bank][:, :])
                    act_.activation(squares[:, j, :], ring_ps[bank][:, :], ACT.Square).then_inc(squares_ready, 1)
                    copy(zh_hi[:, j, :], ring_ps[bank][:, :],
                         scale=consts[:, ROW_GFFN + j:ROW_GFFN + j + 1]).then_inc(h_hi_ready, 1)

            def split_hi_f(m, n, use):
                act_.wait_ge(raw_loaded[m], 16 * (use + 1))
                act_.wait_ge(block_done, done(n - RING_F))
                copy(w_hi[m][:, :], raw[m][:, :]).then_inc(hi_ready, 1)

            first_f = N_F // RING

            def gate_conv(p, par):
                for g in range(2):
                    f = 2 * p + g
                    col = lambda row: consts[:, bass.ds(row + f, 1)]
                    act_.wait_ge(evacuated[2 + g], read_out(USES_F + p))
                    act_.activation(fconv[:, 2 * par + g, :], fg[:, g, 2:S + 2], ACT.Identity,
                                    scale=col(ROW_FCONV + 2 * NF), bias=col(ROW_FBIAS)).then_inc(ftap, 1)

            def gate_silu(p, par):
                for g in range(2):
                    act_.wait_ge(ftaps_dve, 4 * p + 3 + g)
                    act_.activation(silu[:, 2 * par + g, :], fconv[:, 2 * par + g, :],
                                    ACT.Silu).then_inc(silu_ready, 1)
                for g in range(2):
                    act_.wait_ge(act_ready, 2 * p + g + 1)
                    copy(ffn_hi[:, 2 * par + g, :], act[:, g, :]).then_inc(a_hi_ready, 1)

            split_hi_f(2, N_F + 2, first_f)
            split_hi_f(0, N_F + 3, first_f + 1)
            gate_conv(0, 0)
            gate_silu(0, 0)

            def pair(p, par):
                split_hi_f(1, N_F + 3 * p + 1, first_f + p)
                split_hi_f(2, N_F + 3 * p + 2, first_f + p)
                gate_conv(p, par)
                return N_F + 3 * p + 3

            with act_.Fori(0, NP // 2 - 1) as i:
                for u, par in ((1, 1), (2, 0)):
                    p = 2 * i + u
                    n = pair(p, par)
                    split_hi_f(0, n, first_f + p + 1)
                    gate_silu(p, par)
            n = pair(NP - 2, 1)
            split_hi_f(0, n, first_f + NP - 1)
            gate_silu(NP - 2, 1)
            pair(NP - 1, 0)
            gate_silu(NP - 1, 0)

            for t in range(TT):
                act_.wait_ge(final_done, t + 1)
                act_.activation(scratch[:, t, :], wide[:, 2 * t:2 * t + 2, :], ACT.Square,
                                accum_out=sums[:, 4 + t:5 + t]).then_inc(sums_ready, 1)
                act_.wait_ge(sums_ready, TT + t + 1)
                copy(means[:, 4 + t:5 + t], sums[:, 4 + t:5 + t], scale=1.0 / D,
                     bias=EPS).then_inc(means_ready, 1)

        @block.vector
        def _(dve):
            as_f32 = lambda ap: ap.bitcast(F32)

            def split_lo(slot, n):
                dve.wait_ge(hi_ready, n + 1)
                dve.tensor_tensor(w_lo[slot][:, :], raw[slot][:, :], as_f32(w_hi[slot][:, :]),
                                  ALU.subtract).then_inc(lo_ready, 1)

            count = [0]

            def step(ins):
                ins.then_inc(angles, 1)
                count[0] += 1

            def after_last():
                dve.wait_ge(angles, count[0])

            pos_f, r, t_, a1, red, mag = (angle[:, i, :] for i in range(6))
            dve.wait_ge(rope_loaded, 32)
            step(dve.tensor_copy(pos_f, pos_i[:, :]))
            after_last()
            step(dve.tensor_scalar(r, pos_f, rope_c[:, 0:1], None, ALU.mult))
            big = 2 * math.pi * 4096
            b1, b2, b3, b4 = cut(big, 12, 3)
            s1, s2, s3, s4 = cut(2 * math.pi, 12, 3)
            after_last()
            step(dve.tensor_scalar(t_, r, 1.0 / big, ROUND, ALU.mult, ALU.add))
            after_last()
            step(dve.tensor_scalar(t_, t_, -ROUND, None, ALU.add))
            after_last()
            step(dve.tensor_scalar(a1, t_, 64 * ROUND, -64 * ROUND, ALU.add, ALU.add))
            after_last()
            step(dve.tensor_tensor(t_, t_, a1, ALU.subtract))
            for const in (b1, b2, b3, b4):
                for count_ in (a1, t_):
                    after_last()
                    step(dve.scalar_tensor_tensor(out=r, in0=count_, scalar=-const, in1=r,
                                                  op0=ALU.mult, op1=ALU.add))
            after_last()
            step(dve.tensor_scalar(t_, r, 1.0 / (2 * math.pi), ROUND, ALU.mult, ALU.add))
            after_last()
            step(dve.tensor_scalar(t_, t_, -ROUND, None, ALU.add))
            for const in (s1, s2, s3, s4):
                after_last()
                step(dve.scalar_tensor_tensor(out=r, in0=t_, scalar=-const, in1=r,
                                              op0=ALU.mult, op1=ALU.add))
            after_last()
            step(dve.tensor_scalar(red, r, PI_IN, -PI_IN, ALU.min, ALU.max))
            after_last()
            step(dve.scalar_tensor_tensor(out=mag, in0=red, scalar=-1.0, in1=red,
                                          op0=ALU.mult, op1=ALU.max))
            assert count[0] == ANGLE_STEPS

            dve.wait_ge(consts_seen, 1)
            dve.tensor_copy(consts[:, :], ring_ps[3][:, 0:P]).then_inc(consts_ready, 1)
            split_lo(0, 0)
            dve.wait_ge(consts_ready, 1)
            for k in range(KD):
                dve.wait_ge(x_hi_ready, 2 * (k // 2) + 2)
                dve.scalar_tensor_tensor(out=xm_lo[:, k, :], in0=wide[:, k // 2, S * (k % 2):S * (k % 2 + 1)],
                                         scalar=consts[:, ROW_GMIX + k:ROW_GMIX + k + 1],
                                         in1=as_f32(xm_hi[:, k, :]), op0=ALU.mult,
                                         op1=ALU.subtract).then_inc(x_lo_ready, 1)
            split_lo(1, 1)
            dve.wait_ge(tables_ready, 2)
            dve.wait_ge(setup, 9)

            with dve.Fori(0, STEPS) as c:
                n0 = PER_STEP * c
                for b in range(PER_STEP):
                    split_lo((b + 2) % RING, n0 + b + 2)
                    if b == B:
                        dve.wait_ge(scores_done, 2 * c + 2)
                        dve.tensor_tensor(masked[:, :, :], wide[:, 0:2, 0:3 * P],
                                          mask[:, None, :].to_broadcast([P, 2, 3 * P]),
                                          ALU.add).then_inc(masked_done, 1)
                        dve.wait_ge(masked_done, 3 * c + 1)
                        for i, at in enumerate((slice(0, P), slice(P, 3 * P))):
                            dve.reduce_max(row_max[:, i:i + 3:2], masked[:, :, at],
                                           mybir.AxisListType.X).then_inc(masked_done, 1)
                        dve.wait_ge(masked_done, 3 * c + 3)
                        dve.tensor_scalar(neg_max[:, :], row_max[:, :], -SCALE, None,
                                          ALU.mult).then_inc(neg_max_ready, 1)
                    if b == GC:
                        dve.wait_ge(exp_done, 4 * c + 4)
                        dve.reciprocal(row_inv[:, :], row_sum[:, :]).then_inc(inv_ready, 1)
                        dve.wait_ge(inv_ready, c + 1)
                        for h in range(2):
                            for i, at in enumerate((slice(0, P), slice(P, 3 * P))):
                                col = 2 * h + i
                                dve.tensor_scalar(probs_n[:, h, at], probs[:, h, at],
                                                  row_inv[:, col:col + 1], None,
                                                  ALU.mult).then_inc(probs_ready, 1)
                    for g in range(2):
                        bank, use = (2 * b + g) % BANKS, 4 * c + (2 * b + g) // BANKS
                        ps = ring_ps[bank]
                        if b in (C, Q, K, B):
                            dve.wait_ge(*((left_done, left(n0 + b)) if g == 0
                                          else (block_done, done(n0 + b))))
                        if b == C:
                            dve.wait_ge(evacuated[g], read_out(4 * c))
                            dve.tensor_tensor(cx[:, g, 2:S + 2], ps[:, :], xs[:, g, :],
                                              ALU.mult).then_inc(evacuated[bank], 1)
                            dve.wait_ge(evacuated[bank], read_out(use))
                            tap = lambda i: consts[:, bass.ds(ROW_CONV + KD * i + 2 * c + g, 1)]
                            so_far = 3 * (2 * c + g)
                            dve.tensor_scalar(conv[:, g, :], cx[:, g, 2:S + 2], tap(2), None,
                                              ALU.mult).then_inc(taps, 1)
                            for i in (1, 0):
                                dve.wait_ge(taps, so_far + 2 - i)
                                dve.scalar_tensor_tensor(out=conv[:, g, :], in0=cx[:, g, i:S + i],
                                                         scalar=tap(i), in1=conv[:, g, :],
                                                         op0=ALU.mult, op1=ALU.add).then_inc(taps, 1)
                        if b in (Q, K):
                            r_ = 2 * (b - Q) + g
                            dve.tensor_tensor(rope_a[:, r_, :], ps[:, :], cosT[:, :], ALU.mult)
                            for to, frm in ((slice(0, 64), slice(64, P)), (slice(64, P), slice(0, 64))):
                                last = dve.tensor_tensor(rope_b[to, r_, :], ps[frm, :], sinT[frm, :],
                                                         ALU.mult)
                            last.then_inc(evacuated[bank], 1)
                        if b == B:
                            dve.wait_ge(taps, 3 * (2 * c + g) + 3)
                            dve.tensor_tensor(z[:, g, :], ps[:, :], conv[:, g, :],
                                              ALU.mult).then_inc(evacuated[bank], 1)
                    if b == GC:
                        for g in range(2):
                            dve.wait_ge(z_hi_ready, 2 * c + g + 1)
                            dve.tensor_tensor(zh_lo[:, bass.ds(2 * c + g, 1), :], z[:, g, :],
                                              as_f32(zh_hi[:, bass.ds(2 * c + g, 1), :]),
                                              ALU.subtract).then_inc(z_lo_ready, 1)
                    if b == GA:
                        dve.wait_ge(attn_hi_ready, c + 1)
                        dve.tensor_tensor(attn_lo[:, bass.ds(2 * c, 2), :], wide[:, 0, :],
                                          as_f32(attn_hi[:, bass.ds(2 * c, 2), :]),
                                          ALU.subtract).then_inc(attn_lo_ready, 1)

            with dve.Fori(0, 2) as i:
                for q in range(4):
                    n = N_D + 4 * i + q
                    split_lo((q + 2) % RING, n + 2)
                    side, gate = (gated_a, gate_a) if q % 2 else (gated_c, gate_c)
                    for g in range(2):
                        bank = 2 * (q % 2) + g
                        dve.wait_ge(*((left_done, left(n)) if g == 0 else (block_done, done(n))))
                        at = q - q % 2 + g
                        dve.scalar_tensor_tensor(out=side[:, at, :], in0=gate[:, bass.ds(4 * i + at, 1), :],
                                                 scalar=1.0, in1=ring_ps[bank][:, :], op0=ALU.add,
                                                 op1=ALU.mult).then_inc(evacuated[bank], 1)
                    if q % 2:
                        for g in range(2):
                            j = 4 * i + q - 1 + g
                            dve.wait_ge(m_hi_ready, j + 1)
                            dve.scalar_tensor_tensor(out=xm_lo[:, bass.ds(j, 1), :],
                                                     in0=merged[:, q - 1 + g, :], scalar=0.5,
                                                     in1=as_f32(xm_hi[:, bass.ds(j, 1), :]), op0=ALU.mult,
                                                     op1=ALU.subtract).then_inc(m_lo_ready, 1)
            for q in range(4):
                split_lo((q + 2) % RING if q < 2 else q - 2, N_E + q + 2)
                for g in range(2):
                    j = 2 * q + g
                    bank = j % BANKS
                    dve.wait_ge(h_hi_ready, j + 1)
                    dve.scalar_tensor_tensor(out=zh_lo[:, j, :], in0=ring_ps[bank][:, :],
                                             scalar=consts[:, ROW_GFFN + j:ROW_GFFN + j + 1],
                                             in1=as_f32(zh_hi[:, j, :]), op0=ALU.mult,
                                             op1=ALU.subtract).then_inc(evacuated[bank], 1)

            dve.wait_ge(stats_done, 1)
            dve.tensor_scalar(means[:, 2:4], wide[:, 3, 0:TT], 1.0 / D, EPS, ALU.mult,
                              ALU.add).then_inc(means_ready, 1)
            dve.wait_ge(rstd_ready, 2)
            for t in range(TT):
                dve.tensor_scalar(diag[:, t, :], ident[:, :], rstd[:, 2 + t:3 + t], None,
                                  ALU.mult).then_inc(diag_ready, 1)
            split_lo(2, N_F + 2)
            dve.wait_ge(bcast_done, 1)
            dve.tensor_copy(rstd_b[:, :], wide[:, 2, 0:S]).then_inc(rstd_b_ready, 1)
            dve.wait_ge(rstd_b_ready, 1)

            def side_done(k, p, g):
                n_left = N_F + 2 * p + k
                n = N_F + k if isinstance(p, int) and p == 0 else N_F + 3 * p - 1 + k
                dve.wait_ge(*((left_done, left(n_left)) if g == 0 else (block_done, done(n))))

            def take_up(p, par):
                for g in range(2):
                    side_done(0, p, g)
                    dve.tensor_tensor(up[:, 2 * par + g, :], ring_ps[g][:, :], rstd_b[:, :],
                                      ALU.mult).then_inc(evacuated[g], 1)

            def take_gate(p, par):
                for g in range(2):
                    side_done(1, p, g)
                    dve.tensor_tensor(fg[:, g, 2:S + 2], ring_ps[2 + g][:, :], rstd_b[:, :],
                                      ALU.mult).then_inc(evacuated[2 + g], 1)
                for i in (1, 0):
                    for g in range(2):
                        f = 2 * p + g
                        if i == 1:
                            dve.wait_ge(ftap, f + 1)
                        else:
                            dve.wait_ge(ftaps_dve, 4 * p + g + 1)
                        dve.scalar_tensor_tensor(out=fconv[:, 2 * par + g, :], in0=fg[:, g, i:S + i],
                                                 scalar=consts[:, bass.ds(ROW_FCONV + NF * i + f, 1)],
                                                 in1=fconv[:, 2 * par + g, :], op0=ALU.mult,
                                                 op1=ALU.add).then_inc(ftaps_dve, 1)

            def act_lo(p, par):
                for g in range(2):
                    dve.wait_ge(a_hi_ready, 2 * p + g + 1)
                    dve.tensor_tensor(ffn_lo[:, 2 * par + g, :], act[:, g, :], as_f32(ffn_hi[:, 2 * par + g, :]),
                                      ALU.subtract).then_inc(a_lo_ready, 1)

            take_up(0, 0)
            split_lo(0, N_F + 3)
            take_gate(0, 0)
            act_lo(0, 0)

            def pair(p, par, more=True):
                split_lo(1, N_F + 3 * p + 1)
                take_up(p, par)
                split_lo(2, N_F + 3 * p + 2)
                take_gate(p, par)
                if more:
                    split_lo(0, N_F + 3 * p + 3)
                act_lo(p, par)

            with dve.Fori(0, NP // 2 - 1) as i:
                pair(2 * i + 1, 1)
                pair(2 * i + 2, 0)
            pair(NP - 2, 1)
            pair(NP - 1, 0, more=False)

            dve.wait_ge(g_final_loaded, 16)
            for t in range(TT):
                dve.wait_ge(rstd_ready, 3 + t)
                for half in range(2):
                    at = slice(512 * half, 512 * (half + 1))
                    dve.scalar_tensor_tensor(out=scratch[:, t, at], in0=wide[:, 2 * t + half, :],
                                             scalar=rstd[:, 4 + t:5 + t], in1=g_final[:, at],
                                             op0=ALU.mult, op1=ALU.mult).then_inc(out_ready, 1)

        @block.tensor
        def _(pe):
            def transpose(to, frm, start=True, stop=True):
                return pe.matmul(to, frm, ident[:, :], start=start, stop=stop, is_transpose=True,
                                 skip_group_check=True)

            def arrived(n):
                pe.wait_ge(lo_ready, n + 1)

            def project(n, bank_at, use, slot, hi, lo, seed=None, before=None, n_left=None, between=None):
                arrived(n)
                whi = w_hi[slot][:, :].rearrange("p (k c) -> p k c", k=KD)
                wlo = w_lo[slot][:, :].rearrange("p (k c) -> p k c", k=KD)
                for g in range(2):
                    bank = (bank_at + g) % BANKS
                    pe.wait_ge(evacuated[bank], free_for(use))
                    to = ring_ps[bank][:, :]
                    if seed:
                        seed(g, ring_ps[bank])
                    for k in range(KD):
                        if before and g == 0:
                            before(k)
                        cols = slice(P * g, P * (g + 1))
                        for i, (w, a) in enumerate(((whi, hi), (whi, lo), (wlo, hi))):
                            last = pe.matmul(to, w[:, k, cols], a[:, k, :],
                                             start=(k == 0 and i == 0 and not seed),
                                             stop=(k == KD - 1 and i == 2), skip_group_check=True)
                    last.then_inc(left_done if g == 0 else block_done, 1)
                    if between and g == 0:
                        between()

            pe.sem_inc(block_done, RING)
            for bank in range(BANKS):
                pe.sem_inc(evacuated[bank], 1)

            pe.wait_ge(setup, 9)
            pe.wait_ge(rows_loaded, 5 * 16)
            transpose(ring_ps[3][:, 0:P], consts_rows[:, :]).then_inc(consts_seen, 1)
            for t in range(TT):
                pe.wait_ge(xn_ready, t + 1)
                for k in range(KD):
                    at = S * (k % 2) + P * t
                    last = transpose(wide[:, k // 2, at:at + P], xn_tok[:, t, P * k:P * (k + 1)])
            last.then_inc(xT_done, 1)
            pe.wait_ge(consts_ready, 1)

            with pe.Fori(0, STEPS) as c:
                for b in range(PER_STEP):
                    n, use = PER_STEP * c + b, 4 * c + 2 * b // BANKS
                    slot, bank_at = b % RING, 2 * b % BANKS
                    if b == V:
                        arrived(n)
                        whi = w_hi[slot][:, :].rearrange("p (k c) -> p k c", k=KD)
                        wlo = w_lo[slot][:, :].rearrange("p (k c) -> p k c", k=KD)
                        for g in range(2):
                            bank = bank_at + g
                            pe.wait_ge(evacuated[bank], free_for(use))
                            for k in range(KD):
                                toks = slice(P * g, P * (g + 1))
                                for i, (a, w) in enumerate(((xm_hi, whi), (xm_lo, whi), (xm_hi, wlo))):
                                    last = pe.matmul(ring_ps[bank][:, :], a[:, k, toks], w[:, k, :],
                                                     start=(k == 0 and i == 0),
                                                     stop=(k == KD - 1 and i == 2))
                            last.then_inc(left_done if g == 0 else block_done, 1)
                        pe.wait_ge(rope_added, 4 * c + 4)
                        for h in range(2):
                            pe.matmul(wide[:, h, 0:P], qkT[:, h, 0:P], qkT[:, 2 + h, 0:P],
                                      start=True, stop=True)
                            pe.matmul(wide[:, h, P:3 * P], qkT[:, h, P:S], qkT[:, 2 + h, :],
                                      start=True, stop=True).then_inc(scores_done, 1)
                    elif b == X:
                        project(n, bank_at, use, slot, xm_hi, xm_lo,
                                before=lambda k: pe.wait_ge(x_lo_ready, k + 1))
                    else:
                        project(n, bank_at, use, slot, xm_hi, xm_lo)
                    if b == GC:
                        pe.wait_ge(probs_ready, 4 * c + 4)
                        for h in range(2):
                            for i in range(3):
                                at = slice(P * i, P * (i + 1))
                                last = transpose(wide[:, 2 + h, at], probs_n[:, h, at])
                            last.then_inc(probsT_done, 1)
                    if b == GA:
                        for h in range(2):
                            pe.wait_ge(probsT_ready, 2 * c + h + 1)
                            cols = slice(HD * h, HD * (h + 1))
                            pe.matmul(wide[:, 0, S * h:S * (h + 1)], v_tok[:, 0, cols],
                                      probsT[:, h, 0:2 * P], start=True, stop=False,
                                      skip_group_check=True)
                            last = pe.matmul(wide[:, 0, S * h + P:S * (h + 1)], v_tok[:, 1, cols],
                                             probsT[:, h, 2 * P:3 * P], start=False, stop=True,
                                             skip_group_check=True)
                        last.then_inc(attn_done, 1)

            pe.wait_ge(z_lo_ready, KD)
            pe.wait_ge(attn_lo_ready, STEPS)
            with pe.Fori(0, 2) as i:
                for q in range(4):
                    hi, lo = (attn_hi, attn_lo) if q % 2 else (zh_hi, zh_lo)
                    project(N_D + 4 * i + q, 2 * (q % 2), N_D * 2 // BANKS + 2 * i + q // 2, q, hi, lo)

            for q in range(4):
                def residual(g, ps, q=q):
                    j = 2 * q + g
                    for t in range(TT):
                        transpose(ps[:, P * t:P * (t + 1)], x_tok[:, t, P * j:P * (j + 1)],
                                  start=(t == 0), stop=False)
                project(N_E + q, 2 * (q % 2), N_E * 2 // BANKS + q // 2, q, xm_hi, xm_lo, seed=residual,
                        before=(lambda k: pe.wait_ge(m_lo_ready, k + 1)) if q == 0 else None)

            def h_ready(k):
                pe.wait_ge(evacuated[k % BANKS], read_out(N_E * 2 // BANKS + k // BANKS))

            def statistics():
                pe.wait_ge(sumsq_ready, KD - 1)
                for t in range(TT):
                    last = pe.matmul(wide[:, 3, t:t + 1], sumsq[:, KD % 2, P * t:P * (t + 1)], ones[:, 0:1],
                                     start=True, stop=True, skip_group_check=True)
                last.then_inc(stats_done, 1)

            def broadcast():
                pe.wait_ge(diag_ready, TT)
                pe.matmul(wide[:, 2, 0:S], ones[:, :], diag[:, :, :], start=True,
                          stop=True).then_inc(bcast_done, 1)

            project(N_F, 0, USES_F, 0, zh_hi, zh_lo, before=h_ready, between=statistics)
            project(N_F + 1, 2, USES_F, 1, zh_hi, zh_lo, between=broadcast)
            pe.wait_ge(h_hi_ready, KD)
            pe.wait_ge(rstd_b_ready, 1)
            for t in range(TT):
                for k in range(KD):
                    transpose(wide[:, 2 * t + k // 4, P * (k % 4):P * (k % 4 + 1)],
                              hT[:, k, P * t:P * (t + 1)], start=(k % 4 == 0), stop=False)

            def down(n, p, par, slot, final=False):
                arrived(n)
                pe.wait_ge(a_lo_ready, 2 * p + 2)
                whi = w_hi[slot][:, :].rearrange("p (g c) -> p g c", g=2)
                wlo = w_lo[slot][:, :].rearrange("p (g c) -> p g c", g=2)
                for t in range(TT):
                    toks = slice(P * t, P * (t + 1))
                    for g in range(2):
                        for i, (a, w) in enumerate(((ffn_hi, whi), (ffn_lo, whi), (ffn_hi, wlo))):
                            for half in range(2):
                                last = pe.matmul(wide[:, 2 * t + half, :], a[:, 2 * par + g, toks],
                                                 w[:, g, 512 * half:512 * (half + 1)], start=False,
                                                 stop=(final and g == 1 and i == 2),
                                                 skip_group_check=True)
                    if final:
                        last.then_inc(final_done, 1)
                if not final:
                    last.then_inc(block_done, 1)

            def pair(p, par):
                project(N_F + 3 * p - 1, 0, USES_F + p, 2, zh_hi, zh_lo)
                project(N_F + 3 * p, 2, USES_F + p, 0, zh_hi, zh_lo)
                down(N_F + 3 * p + 1, p - 1, 1 - par, 1)

            with pe.Fori(0, NP // 2) as i:
                pair(2 * i + 1, 1)
                pair(2 * i + 2, 0)
            down(N_F + 3 * NP - 1, NP - 1, 0, 2, final=True)


_INS = ["x", "positions", "norm_mix_g", "w_in", "conv_w", "w_conv_out", "w_attn_out", "w_out", "norm_ffn_g",
        "w_ffn_in", "ffn_conv_w", "ffn_conv_b", "w_ffn_down", "norm_final_g"]


def kernel(**inputs):
    import concourse.bacc as bacc
    from concourse.bass_utils import run_bass_kernel_spmd

    nc = bacc.Bacc("TRN2", target_bir_lowering=False, num_devices=1)
    arrays = {f"in_{name}": np.ascontiguousarray(inputs[name]) for name in _INS}
    half = np.exp(np.float32(-math.log(10000.0)) * np.arange(HD // 2, dtype=np.float32) * np.float32(2.0 / HD))
    cols = np.stack([np.tile(half, 2), np.repeat([1.0, -1.0], HD // 2), np.full(HD, math.pi / 2)], axis=1)
    arrays["in_rope_cols"] = np.ascontiguousarray(cols.astype(np.float32))
    args = [nc.dram_tensor(n, a.shape, mybir.dt.from_np(a.dtype), kind="ExternalInput").ap()
            for n, a in arrays.items()]
    out = nc.dram_tensor("out", (1, S, D), F32, kind="ExternalOutput").ap()
    layer(nc, *args, out)
    result = run_bass_kernel_spmd(nc, [arrays], core_ids=[0])
    return result.results[0]["out"]
```

```python
import math
from contextlib import ExitStack

import numpy as np
import concourse.bass as bass
from concourse import mybir

F32 = mybir.dt.float32
F32R = mybir.dt.float32r
I32 = mybir.dt.int32
ALU = mybir.AluOpType
ACT = mybir.ActivationFunctionType

P = 128
D = 1024
S = 256
TT = S // P
KD = D // P
HD = 128
DFF = 2816
NF = DFF // P
NP = NF // 2
BLK = 2048
COLS = BLK // KD
EPS = 1e-6
SCALE = HD ** -0.5
NEG = -1e30
RING = 4
RING_F = 3
BANKS = 4
STEPS = 4
PER_STEP = 8
N_D = STEPS * PER_STEP
N_E = N_D + 8
N_F = N_E + 4
USES_F = 2 * N_F // BANKS

X, C, Q, K, V, B, GC, GA = range(PER_STEP)
W_IN_PART = {X: 2, C: 1, Q: 3, K: 4, V: 5, B: 0, GC: 6, GA: 7}

ROW_CONV = 0
ROW_FCONV = ROW_CONV + 3 * KD
ROW_FBIAS = ROW_FCONV + 3 * NF
ROW_GMIX = ROW_FBIAS + NF
ROW_GFFN = ROW_GMIX + KD
assert ROW_GFFN + KD == P

ROUND = 1.5 * 2.0 ** 23
PI_IN = 3.1415925
ANGLE_STEPS = 18


def cut(value, bits, parts):
    out = []
    for _ in range(parts):
        e = math.floor(math.log2(abs(value))) - bits + 1
        out.append(math.floor(value / 2.0 ** e) * 2.0 ** e)
        value -= out[-1]
    return out + [float(np.float32(value))]


def layer(nc, x, positions, norm_mix_g, w_in, conv_w, w_conv_out, w_attn_out, w_out, norm_ffn_g,
          w_ffn_in, ffn_conv_w, ffn_conv_b, w_ffn_down, norm_final_g, rope_cols, out):
    rows = lambda w: w[0].rearrange("(k p) n -> p k n", p=P)
    w_in_v, w_conv_out_v, w_attn_out_v, w_out_v, w_ffn_in_v, w_ffn_down_v = map(
        rows, (w_in, w_conv_out, w_attn_out, w_out, w_ffn_in, w_ffn_down))
    x_v = x[0].rearrange("(t p) d -> p t d", p=P)
    out_v = out[0].rearrange("(t p) d -> p t d", p=P)

    ctx = ExitStack()
    with ctx:
        sb = lambda name, shape, dt=F32: ctx.enter_context(nc.sbuf_tensor(name, shape, dt))
        sem = lambda name: ctx.enter_context(nc.semaphore(name))

        raw = [sb(f"raw{i}", [P, BLK]) for i in range(RING)]
        w_hi = [sb(f"w_hi{i}", [P, BLK], F32R) for i in range(RING)]
        w_lo = [sb(f"w_lo{i}", [P, BLK], F32R) for i in range(RING)]
        xm_hi, xm_lo = sb("xm_hi", [P, KD, S], F32R), sb("xm_lo", [P, KD, S], F32R)
        zh_hi, zh_lo = sb("zh_hi", [P, KD, S], F32R), sb("zh_lo", [P, KD, S], F32R)
        attn_hi, attn_lo = sb("attn_hi", [P, KD, S], F32R), sb("attn_lo", [P, KD, S], F32R)
        ffn_hi, ffn_lo = attn_hi, attn_lo
        x_tok = sb("x_tok", [P, TT, D])
        scratch = sb("scratch", [P, TT, D])
        xn_tok = scratch
        gate_c, gate_a = sb("gate_c", [P, KD, S]), sb("gate_a", [P, KD, S])
        hT = gate_c
        consts_rows = sb("consts_rows", [P, P])
        consts = sb("consts", [P, P])
        ident, ones = sb("ident", [P, P]), sb("ones", [P, P])
        mask = sb("mask", [P, 3 * P])
        cosT, sinT = sb("cosT", [P, S]), sb("sinT", [P, S])
        rope_c = sb("rope_c", [P, 3])
        xs = sb("xs", [P, 2, S])
        cx = sb("cx", [P, 2, S + 2])
        conv = sb("conv", [P, 2, S])
        z = conv
        rope_a, rope_b = sb("rope_a", [P, 4, S]), sb("rope_b", [P, 4, S])
        qkT = sb("qkT", [P, 4, S])
        v_tok = sb("v_tok", [P, TT, 2 * HD])
        flat = scratch[:, :, :].rearrange("p t d -> p (t d)")
        masked = flat[:, 0:6 * P].rearrange("p (h s) -> p h s", h=2)
        probs = flat[:, 6 * P:12 * P].rearrange("p (h s) -> p h s", h=2)
        probs_n = masked
        probsT = sb("probsT", [P, 2, 3 * P])
        row_max, neg_max = sb("row_max", [P, 4]), sb("neg_max", [P, 4])
        row_sum, row_inv = sb("row_sum", [P, 4]), sb("row_inv", [P, 4])
        gated_c, gated_a = rope_a, rope_b
        merged = qkT
        up, silu = rope_a, rope_b
        fg = sb("fg", [P, 2, S + 2])
        fconv = qkT
        act = z
        sumsq = xs
        spare = gate_a[:, :, :].rearrange("p j s -> p (j s)")
        g_final = spare[:, 0:D]
        diag = spare[:, D:D + S].rearrange("p (t s) -> p t s", t=TT)
        rstd_b = spare[:, D + S:D + 2 * S]
        sums = sb("sums", [P, 8])
        means = sb("means", [P, 8])
        rstd = sb("rstd", [P, 8])
        minus_half = sb("minus_half", [P, 2])
        pos_i = rope_a[:, 0, :].bitcast(I32)
        angle = gate_a

        ring_ps = [ctx.enter_context(nc.psum_tensor(f"ring_ps{i}", [P, 2 * S], F32))[:, 0:S]
                   for i in range(BANKS)]
        wide = ctx.enter_context(nc.psum_tensor("wide", [P, 4, 512], F32))

        x_loaded = [sem(f"x_loaded{t}") for t in range(TT)]
        rows_loaded = sem("rows_loaded")
        rope_loaded = sem("rope_loaded")
        g_final_loaded = sem("g_final_loaded")
        raw_loaded = [sem(f"raw_loaded{i}") for i in range(RING)]
        hi_ready = sem("hi_ready")
        lo_ready = sem("lo_ready")
        slots_seen = sem("slots_seen")
        first_input = sem("first_input")
        left_hi_ready = sem("left_hi_ready")
        left_lo_ready = sem("left_lo_ready")
        left_done = sem("left_done")
        block_done = sem("block_done")
        evacuated = [sem(f"evacuated{i}") for i in range(BANKS)]
        setup = sem("setup")
        pool_steps = sem("pool_steps")
        sums_ready = sem("sums_ready")
        means_ready = sem("means_ready")
        rstd_ready = sem("rstd_ready")
        xn0_ready, xn1_ready = sem("xn0_ready"), sem("xn1_ready")
        consts_seen = sem("consts_seen")
        consts_ready = sem("consts_ready")
        xT_done = sem("xT_done")
        x_hi_ready, x_lo_ready = sem("x_hi_ready"), sem("x_lo_ready")
        angles = sem("angles")
        tables_ready = sem("tables_ready")
        taps = sem("taps")
        z_hi_ready, z_lo_ready = sem("z_hi_ready"), sem("z_lo_ready")
        rope_added = sem("rope_added")
        scores_done, masked_done = sem("scores_done"), sem("masked_done")
        neg_max_ready, exp_done = sem("neg_max_ready"), sem("exp_done")
        inv_ready, probs_ready = sem("inv_ready"), sem("probs_ready")
        probsT_done, probsT_ready = sem("probsT_done"), sem("probsT_ready")
        attn_done = sem("attn_done")
        attn_hi_ready, attn_lo_ready = sem("attn_hi_ready"), sem("attn_lo_ready")
        merged_ready = sem("merged_ready")
        m_hi_ready, m_lo_ready = sem("m_hi_ready"), sem("m_lo_ready")
        squares_ready, sumsq_ready = sem("squares_ready"), sem("sumsq_ready")
        h_hi_ready = sem("h_hi_ready")
        stats_done, diag_ready, bcast_done = sem("stats_done"), sem("diag_ready"), sem("bcast_done")
        rstd_b_ready = sem("rstd_b_ready")
        ftap, ftaps_dve = sem("ftap"), sem("ftaps_dve")
        silu_ready, act_ready = sem("silu_ready"), sem("act_ready")
        a_hi_ready, a_lo_ready = sem("a_hi_ready"), sem("a_lo_ready")
        final_done = sem("final_done")
        half_mean = sem("half_mean")
        gained = sem("gained")
        left_out_ready, right_out_ready = sem("left_out_ready"), sem("right_out_ready")
        out_stored = sem("out_stored")

        left = lambda n: n + 1
        done = lambda n: n + 1 + RING
        slot_free = lambda n: done(n - RING)
        free_for = lambda k: k + 1
        read_out = lambda k: k + 2

        block = ctx.enter_context(nc.Block())

        @block.sync
        def _(sp):
            def load(slot, use, n, source):
                if n is not None:
                    sp.wait_ge(lo_ready, n - RING + 1)
                    sp.sem_inc(slots_seen, 1)
                sp.dma_start(raw[slot][:, :].rearrange("p (k c) -> p k c", k=source.shape[1]),
                             source).then_inc(raw_loaded[slot], 16)

            part = lambda b, c: w_in_v[:, :, bass.ds(W_IN_PART[b] * D + COLS * c, COLS)]
            for t in range(TT):
                sp.dma_start(x_tok[:, t, :], x_v[:, t, :]).then_inc(x_loaded[t], 16)
            at = 0
            for source in (conv_w[0].rearrange("i (j p) -> (i j) p", p=P),
                           ffn_conv_w[0].rearrange("i (j p) -> (i j) p", p=P),
                           ffn_conv_b[0].rearrange("(j p) -> j p", p=P),
                           norm_mix_g[0].rearrange("(j p) -> j p", p=P),
                           norm_ffn_g[0].rearrange("(j p) -> j p", p=P)):
                sp.dma_start(consts_rows[at:at + source.shape[0], :], source).then_inc(rows_loaded, 16)
                at += source.shape[0]
            for b in range(RING):
                load(b, 0, None, part(b, 0))
            with sp.Fori(0, STEPS - 1) as c:
                for b in range(RING, PER_STEP):
                    load(b % RING, None, PER_STEP * c + b, part(b, c))
                for b in range(RING):
                    load(b, None, PER_STEP * c + b + PER_STEP, part(b, c + 1))
            for b in range(RING, PER_STEP):
                load(b % RING, None, PER_STEP * (STEPS - 1) + b, part(b, STEPS - 1))
            for j in range(4):
                for i, source in enumerate((w_conv_out_v, w_attn_out_v)):
                    n = N_D + 2 * j + i
                    load(n % RING, None, n, source[:, :, COLS * j:COLS * (j + 1)])
            for j in range(4):
                load(j, None, N_E + j, w_out_v[:, :, COLS * j:COLS * (j + 1)])

            def load_f(m, n_split, source):
                sp.wait_ge(lo_ready, n_split)
                sp.sem_inc(slots_seen, 1)
                sp.dma_start(raw[m][:, :].rearrange("p (k c) -> p k c", k=source.shape[1]),
                             source).then_inc(raw_loaded[m], 16)

            up_cols = lambda p: w_ffn_in_v[:, :, bass.ds(COLS * p, COLS)]
            gate_cols = lambda p: w_ffn_in_v[:, :, bass.ds(DFF + COLS * p, COLS)]
            down_rows = lambda p: w_ffn_down_v[:, bass.ds(2 * p, 2), :]
            load_f(0, N_F - 3, up_cols(0))
            load_f(1, N_F - 2, gate_cols(0))
            load_f(2, N_F - 1, up_cols(1))
            load_f(0, N_F + 1, gate_cols(1))
            load_f(1, N_F + 2, down_rows(0))
            with sp.Fori(2, NP) as p:
                load_f(2, N_F + 3 * p - 3, up_cols(p))
                load_f(0, N_F + 3 * p - 2, gate_cols(p))
                load_f(1, N_F + 3 * p - 1, down_rows(p - 1))
            load_f(2, N_F + 3 * NP - 3, down_rows(NP - 1))

            for i in range(2 * TT):
                t, half = divmod(i, 2)
                sp.wait_ge(right_out_ready if half else left_out_ready, t + 1)
                sp.dma_start(out_v[:, t, 512 * half:512 * (half + 1)],
                             scratch[:, t, 512 * half:512 * (half + 1)]).then_inc(out_stored, 16)
            sp.wait_ge(out_stored, 16 * 2 * TT)

        @block.gpsimd
        def _(pool):
            pool.dma_start(pos_i[:, :], positions.to_broadcast([P, S])).then_inc(rope_loaded, 16)
            pool.dma_start(rope_c[:, :], rope_cols).then_inc(rope_loaded, 16)
            pool.memset(ident[:, :], 0.0).then_inc(setup, 1)
            pool.memset(mask[:, :], 0.0).then_inc(setup, 1)
            pool.memset(minus_half[:, :], -0.5).then_inc(setup, 1)
            pool.wait_ge(setup, 3)
            pool.affine_select(out=ident[:, :], in_=ident[:, :], compare_op=ALU.not_equal, fill=1.0,
                               base=0, pattern=[[-1, P]], channel_multiplier=1).then_inc(setup, 1)
            for tile, at in enumerate((slice(0, P), slice(P, 3 * P))):
                pool.affine_select(out=mask[:, at], in_=mask[:, at], compare_op=ALU.is_ge, fill=NEG,
                                   base=P * tile, pattern=[[-1, P * (tile + 1)]],
                                   channel_multiplier=1).then_inc(setup, 1)
            pool.memset(ones[:, :], 1.0).then_inc(setup, 1)
            pool.memset(cx[:, :, 0:2], 0.0).then_inc(setup, 1)
            pool.memset(fg[:, :, 0:2], 0.0).then_inc(setup, 1)

            def inverse_root(at):
                pool.tensor_tensor(rstd[:, at:at + 2], means[:, at:at + 2], minus_half[:, :],
                                   ALU.pow).then_inc(rstd_ready, 1)

            pool.wait_ge(means_ready, 1)
            inverse_root(0)

            with pool.Fori(0, STEPS) as c:
                for r in range(4):
                    bank, use = r % BANKS, 4 * c + 1
                    pool.wait_ge(evacuated[bank], read_out(use))
                    pool.tensor_tensor(qkT[:, r, :], rope_a[:, r, :], rope_b[:, r, :],
                                       ALU.add).then_inc(rope_added, 1)

            with pool.Fori(0, 2) as i:
                for u in range(2):
                    for g in range(2):
                        pool.wait_ge(evacuated[2 + g], read_out(2 * N_D // BANKS + 2 * i + u))
                        pool.tensor_tensor(merged[:, 2 * u + g, :], gated_c[:, 2 * u + g, :],
                                           gated_a[:, 2 * u + g, :], ALU.add).then_inc(merged_ready, 1)

            pool.wait_ge(m_lo_ready, KD)
            pool.dma_start(g_final[:, :], norm_final_g.rearrange("(a n) -> a n", a=1)
                           .to_broadcast([P, D])).then_inc(g_final_loaded, 16)

            squares = scratch[:, :, :].rearrange("p t (j s) -> p (t j) s", s=S)
            for j in range(1, KD):
                pool.wait_ge(squares_ready, j + 1)
                if j > 1:
                    pool.wait_ge(sumsq_ready, j - 1)
                before = squares[:, 0, :] if j == 1 else sumsq[:, j % 2, :]
                pool.tensor_tensor(sumsq[:, (j + 1) % 2, :], before, squares[:, j, :],
                                   ALU.add).then_inc(sumsq_ready, 1)
            pool.wait_ge(means_ready, 2)
            inverse_root(2)

            def times_up(p, par):
                for g in range(2):
                    pool.wait_ge(silu_ready, 2 * p + g + 1)
                    pool.tensor_tensor(act[:, g, :], silu[:, 2 * par + g, :], up[:, 2 * par + g, :],
                                       ALU.mult).then_inc(act_ready, 1)

            times_up(0, 0)
            with pool.Fori(0, NP // 2) as i:
                times_up(2 * i + 1, 1)
                times_up(2 * i + 2, 0)
            for t in range(TT):
                pool.wait_ge(means_ready, 3 + t)
                pool.tensor_tensor(rstd[:, 4 + t:5 + t], means[:, 6 + t:7 + t], minus_half[:, 0:1],
                                   ALU.pow).then_inc(rstd_ready, 1)

        @block.scalar
        def _(act_):
            copy = lambda out_, in_, **k: act_.activation(out_, in_, ACT.Copy, **k)

            def hi_side(side):
                at = lambda w: w[0][:, :].rearrange("p (k c) -> p k c", k=KD)[:, :, P * side:P * (side + 1)]
                copy(at(w_hi), at(raw)).then_inc(hi_ready if side else left_hi_ready, 1)

            def split_hi(slot, use, n, free):
                act_.wait_ge(raw_loaded[slot], 16 * (use + 1))
                act_.wait_ge(block_done, free)
                copy(w_hi[slot][:, :], raw[slot][:, :]).then_inc(hi_ready, 1)

            act_.wait_ge(first_input, 1)
            act_.activation(sums[:, 7:8], sums[:, 6:7], ACT.Square)
            for t in range(TT):
                act_.wait_ge(x_loaded[t], 16)
                act_.activation(xn_tok[:, t, :], x_tok[:, t, :], ACT.Square,
                                accum_out=sums[:, t:t + 1]).then_inc(sums_ready, 1)
            act_.wait_ge(sums_ready, TT)
            copy(means[:, 0:2], sums[:, 0:2], scale=1.0 / D, bias=EPS).then_inc(means_ready, 1)
            act_.wait_ge(rstd_ready, 1)
            copy(xn_tok[:, 0, :], x_tok[:, 0, :], scale=rstd[:, 0:1]).then_inc(xn0_ready, 1)
            act_.wait_ge(raw_loaded[0], 16)
            hi_side(0)
            act_.wait_ge(consts_seen, 1)
            copy(consts[:, :], ring_ps[3][:, 0:P]).then_inc(consts_ready, 1)
            act_.wait_ge(consts_ready, 1)
            act_.wait_ge(xT_done, 1)
            for k in range(KD):
                copy(xm_hi[:, k, :], wide[:, k // 2, S * (k % 2):S * (k % 2 + 1)],
                     scale=consts[:, ROW_GMIX + k:ROW_GMIX + k + 1]).then_inc(x_hi_ready, 1)
            hi_side(1)
            split_hi(1, 0, 1, slot_free(1))
            act_.wait_ge(angles, ANGLE_STEPS)
            act_.activation(sinT[:, :], angle[:, 3, :], ACT.Sin,
                            scale=rope_c[:, 1:2]).then_inc(tables_ready, 1)
            act_.activation(cosT[:, :], angle[:, 4, :], ACT.Sin, scale=-1.0,
                            bias=rope_c[:, 2:3]).then_inc(tables_ready, 1)

            with act_.Fori(0, STEPS) as c:
                n0 = PER_STEP * c
                for b in range(PER_STEP):
                    if b == GA:
                        for h in range(2):
                            act_.wait_ge(probsT_done, 2 * c + h + 1)
                            copy(probsT[:, h, :], wide[:, 2 + h, 0:3 * P]).then_inc(probsT_ready, 1)
                    ahead = b + 2
                    if ahead == PER_STEP:
                        act_.wait_ge(raw_loaded[0], 16 * (2 * c + 3))
                        act_.wait_ge(block_done, slot_free(n0 + ahead))
                        hi_side(0)
                        hi_side(1)
                    else:
                        split_hi(ahead % RING, 2 * c + ahead // RING, n0 + ahead, slot_free(n0 + ahead))
                    for g in range(2):
                        bank = (2 * b + g) % BANKS
                        if b in (X, V, GC, GA):
                            act_.wait_ge(*((left_done, left(n0 + b)) if g == 0
                                           else (block_done, done(n0 + b))))
                        if b == X:
                            copy(xs[:, g, :], ring_ps[bank][:, :]).then_inc(evacuated[bank], 1)
                        if b == V:
                            copy(v_tok[:, g, :], ring_ps[bank][:, :]).then_inc(evacuated[bank], 1)
                        if b in (GC, GA):
                            gate = gate_c if b == GC else gate_a
                            act_.activation(gate[:, bass.ds(2 * c + g, 1), :], ring_ps[bank][:, :],
                                            ACT.Tanh, scale=0.5).then_inc(evacuated[bank], 1)
                    if b == B:
                        for h in range(2):
                            act_.wait_ge(neg_max_ready, c + 1)
                            for i, at in enumerate((slice(0, P), slice(P, 3 * P))):
                                col = 2 * h + i
                                act_.activation(probs[:, h, at], masked[:, h, at], ACT.Exp,
                                                bias=neg_max[:, col:col + 1], scale=SCALE,
                                                accum_out=row_sum[:, col:col + 1]).then_inc(exp_done, 1)
                        for g in range(2):
                            bank = (2 * b + g) % BANKS
                            act_.wait_ge(evacuated[bank], read_out(4 * c + (2 * b + g) // BANKS))
                            copy(zh_hi[:, bass.ds(2 * c + g, 1), :], z[:, g, :]).then_inc(z_hi_ready, 1)
                    if b == GA:
                        act_.wait_ge(attn_done, c + 1)
                        copy(attn_hi[:, bass.ds(2 * c, 2), :], wide[:, 0, :]).then_inc(attn_hi_ready, 1)

            with act_.Fori(0, 2) as i:
                for q in range(4):
                    ahead = q + 2
                    n = N_D + 4 * i + ahead
                    split_hi(ahead % RING, N_D // RING + i + ahead // RING, n, slot_free(n))
                    if q % 2:
                        for g in range(2):
                            j = 4 * i + q - 1 + g
                            act_.wait_ge(merged_ready, j + 1)
                            copy(xm_hi[:, bass.ds(j, 1), :], merged[:, q - 1 + g, :],
                                 scale=0.5).then_inc(m_hi_ready, 1)
            squares = scratch[:, :, :].rearrange("p t (j s) -> p (t j) s", s=S)
            for q in range(4):
                n = N_E + q + 2
                if q < 2:
                    split_hi((q + 2) % RING, N_E // RING, n, slot_free(n))
                else:
                    split_hi(q - 2, N_F // RING, n, slot_free(n))
                for g in range(2):
                    j = 2 * q + g
                    bank = j % BANKS
                    act_.wait_ge(*((left_done, left(N_E + q)) if g == 0 else (block_done, done(N_E + q))))
                    copy(hT[:, j, :], ring_ps[bank][:, :])
                    act_.activation(squares[:, j, :], ring_ps[bank][:, :], ACT.Square).then_inc(squares_ready, 1)
                    copy(zh_hi[:, j, :], ring_ps[bank][:, :],
                         scale=consts[:, ROW_GFFN + j:ROW_GFFN + j + 1]).then_inc(h_hi_ready, 1)

            def split_hi_f(m, n, use):
                act_.wait_ge(raw_loaded[m], 16 * (use + 1))
                act_.wait_ge(block_done, done(n - RING_F))
                copy(w_hi[m][:, :], raw[m][:, :]).then_inc(hi_ready, 1)

            first_f = N_F // RING

            def gate_conv(p, par):
                for g in range(2):
                    f = 2 * p + g
                    col = lambda row: consts[:, bass.ds(row + f, 1)]
                    act_.wait_ge(evacuated[2 + g], read_out(USES_F + p))
                    act_.activation(fconv[:, 2 * par + g, :], fg[:, g, 2:S + 2], ACT.Identity,
                                    scale=col(ROW_FCONV + 2 * NF), bias=col(ROW_FBIAS)).then_inc(ftap, 1)

            def gate_silu(p, par):
                for g in range(2):
                    act_.wait_ge(ftaps_dve, 4 * p + 3 + g)
                    act_.activation(silu[:, 2 * par + g, :], fconv[:, 2 * par + g, :],
                                    ACT.Silu).then_inc(silu_ready, 1)
                for g in range(2):
                    act_.wait_ge(act_ready, 2 * p + g + 1)
                    copy(ffn_hi[:, 2 * par + g, :], act[:, g, :]).then_inc(a_hi_ready, 1)

            split_hi_f(2, N_F + 2, first_f)
            split_hi_f(0, N_F + 3, first_f + 1)
            gate_conv(0, 0)
            gate_silu(0, 0)

            def pair(p, par):
                split_hi_f(1, N_F + 3 * p + 1, first_f + p)
                split_hi_f(2, N_F + 3 * p + 2, first_f + p)
                gate_conv(p, par)
                return N_F + 3 * p + 3

            with act_.Fori(0, NP // 2 - 1) as i:
                for u, par in ((1, 1), (2, 0)):
                    p = 2 * i + u
                    n = pair(p, par)
                    split_hi_f(0, n, first_f + p + 1)
                    gate_silu(p, par)
            n = pair(NP - 2, 1)
            split_hi_f(0, n, first_f + NP - 1)
            gate_silu(NP - 2, 1)
            pair(NP - 1, 0)
            gate_silu(NP - 1, 0)

            unused = gate_c[:, :, :].rearrange("p j s -> p (j s)")
            for t in range(TT):
                for half in range(2):
                    i = 2 * t + half
                    act_.wait_ge(final_done, i + 1)
                    act_.activation(unused[:, 512 * i:512 * (i + 1)], wide[:, i, :], ACT.Square,
                                    accum_out=sums[:, 4 + i:5 + i]).then_inc(sums_ready, 1)
                    act_.wait_ge(sums_ready, TT + i + 1)
                    if half == 0:
                        copy(means[:, 4 + t:5 + t], sums[:, 4 + i:5 + i], scale=1.0 / D,
                             bias=EPS).then_inc(half_mean, 1)
                    else:
                        act_.wait_ge(half_mean, t + 1)
                        act_.activation(means[:, 6 + t:7 + t], sums[:, 4 + i:5 + i], ACT.Identity,
                                        scale=1.0 / D, bias=means[:, 4 + t:5 + t]).then_inc(means_ready, 1)
                act_.wait_ge(rstd_ready, 3 + t)
                act_.wait_ge(gained, 2 * t + 1)
                copy(scratch[:, t, 0:512], scratch[:, t, 0:512],
                     scale=rstd[:, 4 + t:5 + t]).then_inc(left_out_ready, 1)

        @block.vector
        def _(dve):
            as_f32 = lambda ap: ap.bitcast(F32)

            def split_lo(slot, n):
                dve.wait_ge(hi_ready, n + 1)
                dve.tensor_tensor(w_lo[slot][:, :], raw[slot][:, :], as_f32(w_hi[slot][:, :]),
                                  ALU.subtract).then_inc(lo_ready, 1)

            def lo_side(slot, side):
                at = lambda w: w[slot][:, :].rearrange("p (k c) -> p k c", k=KD)[:, :, P * side:P * (side + 1)]
                dve.tensor_tensor(at(w_lo), at(raw), as_f32(at(w_hi)),
                                  ALU.subtract).then_inc(lo_ready if side else left_lo_ready, 1)

            count = [0]

            def step(ins):
                ins.then_inc(angles, 1)
                count[0] += 1

            def after_last():
                dve.wait_ge(angles, count[0])

            dve.memset(sums[:, 6:7], 0.0).then_inc(first_input, 1)
            r, t_, a1, red, mag = (angle[:, i, :] for i in range(5))
            dve.wait_ge(rope_loaded, 32)
            step(dve.tensor_scalar(r, pos_i[:, :], rope_c[:, 0:1], None, ALU.mult))
            big = 2 * math.pi * 4096
            b1, b2, b3 = cut(big, 12, 2)
            s1, s2, s3 = cut(2 * math.pi, 12, 2)
            after_last()
            step(dve.tensor_scalar(t_, r, 1.0 / big, ROUND, ALU.mult, ALU.add))
            after_last()
            step(dve.tensor_scalar(t_, t_, -ROUND, None, ALU.add))
            after_last()
            step(dve.tensor_scalar(a1, t_, 64 * ROUND, -64 * ROUND, ALU.add, ALU.add))
            after_last()
            step(dve.tensor_tensor(t_, t_, a1, ALU.subtract))
            for const in (b1, b2, b3):
                for count_ in (a1, t_):
                    after_last()
                    step(dve.scalar_tensor_tensor(out=r, in0=count_, scalar=-const, in1=r,
                                                  op0=ALU.mult, op1=ALU.add))
            dve.wait_ge(rstd_ready, 1)
            dve.tensor_scalar(xn_tok[:, 1, :], x_tok[:, 1, :], rstd[:, 1:2], None,
                              ALU.mult).then_inc(xn1_ready, 1)
            after_last()
            step(dve.tensor_scalar(t_, r, 1.0 / (2 * math.pi), ROUND, ALU.mult, ALU.add))
            after_last()
            step(dve.tensor_scalar(t_, t_, -ROUND, None, ALU.add))
            for const in (s1, s2, s3):
                after_last()
                step(dve.scalar_tensor_tensor(out=r, in0=t_, scalar=-const, in1=r,
                                              op0=ALU.mult, op1=ALU.add))
            after_last()
            step(dve.tensor_scalar(red, r, PI_IN, -PI_IN, ALU.min, ALU.max))
            step(dve.scalar_tensor_tensor(out=mag, in0=r, scalar=-1.0, in1=r, op0=ALU.mult, op1=ALU.max))
            assert count[0] == ANGLE_STEPS

            dve.wait_ge(left_hi_ready, 1)
            lo_side(0, 0)
            dve.wait_ge(consts_ready, 1)
            for k in range(KD):
                dve.wait_ge(x_hi_ready, 2 * (k // 2) + 2)
                dve.scalar_tensor_tensor(out=xm_lo[:, k, :], in0=wide[:, k // 2, S * (k % 2):S * (k % 2 + 1)],
                                         scalar=consts[:, ROW_GMIX + k:ROW_GMIX + k + 1],
                                         in1=as_f32(xm_hi[:, k, :]), op0=ALU.mult,
                                         op1=ALU.subtract).then_inc(x_lo_ready, 1)
            dve.wait_ge(hi_ready, 1)
            lo_side(0, 1)
            split_lo(1, 1)
            dve.wait_ge(tables_ready, 2)
            dve.wait_ge(setup, 9)

            with dve.Fori(0, STEPS) as c:
                n0 = PER_STEP * c
                for b in range(PER_STEP):
                    def split_ahead():
                        if b + 2 == PER_STEP:
                            dve.wait_ge(hi_ready, n0 + b + 3)
                            lo_side(0, 0)
                            lo_side(0, 1)
                        else:
                            split_lo((b + 2) % RING, n0 + b + 2)

                    if b != GC:
                        split_ahead()
                    if b == B:
                        dve.wait_ge(scores_done, 2 * c + 2)
                        dve.tensor_tensor(masked[:, :, :], wide[:, 0:2, 0:3 * P],
                                          mask[:, None, :].to_broadcast([P, 2, 3 * P]),
                                          ALU.add).then_inc(masked_done, 1)
                        dve.wait_ge(masked_done, 3 * c + 1)
                        for i, at in enumerate((slice(0, P), slice(P, 3 * P))):
                            dve.reduce_max(row_max[:, i:i + 3:2], masked[:, :, at],
                                           mybir.AxisListType.X).then_inc(masked_done, 1)
                        dve.wait_ge(masked_done, 3 * c + 3)
                        dve.tensor_scalar(neg_max[:, :], row_max[:, :], -SCALE, None,
                                          ALU.mult).then_inc(neg_max_ready, 1)
                    if b == GC:
                        dve.wait_ge(exp_done, 4 * c + 4)
                        dve.reciprocal(row_inv[:, :], row_sum[:, :]).then_inc(inv_ready, 1)
                        dve.wait_ge(inv_ready, c + 1)
                        for h in range(2):
                            for i, at in enumerate((slice(0, P), slice(P, 3 * P))):
                                col = 2 * h + i
                                dve.tensor_scalar(probs_n[:, h, at], probs[:, h, at],
                                                  row_inv[:, col:col + 1], None,
                                                  ALU.mult).then_inc(probs_ready, 1)
                        split_ahead()
                    for g in range(2):
                        bank, use = (2 * b + g) % BANKS, 4 * c + (2 * b + g) // BANKS
                        ps = ring_ps[bank]
                        if b in (C, Q, K, B):
                            dve.wait_ge(*((left_done, left(n0 + b)) if g == 0
                                          else (block_done, done(n0 + b))))
                        if b == C:
                            dve.wait_ge(evacuated[g], read_out(4 * c))
                            dve.tensor_tensor(cx[:, g, 2:S + 2], ps[:, :], xs[:, g, :],
                                              ALU.mult).then_inc(evacuated[bank], 1)
                            dve.wait_ge(evacuated[bank], read_out(use))
                            tap = lambda i: consts[:, bass.ds(ROW_CONV + KD * i + 2 * c + g, 1)]
                            so_far = 3 * (2 * c + g)
                            dve.tensor_scalar(conv[:, g, :], cx[:, g, 2:S + 2], tap(2), None,
                                              ALU.mult).then_inc(taps, 1)
                            for i in (1, 0):
                                dve.wait_ge(taps, so_far + 2 - i)
                                dve.scalar_tensor_tensor(out=conv[:, g, :], in0=cx[:, g, i:S + i],
                                                         scalar=tap(i), in1=conv[:, g, :],
                                                         op0=ALU.mult, op1=ALU.add).then_inc(taps, 1)
                        if b in (Q, K):
                            r_ = 2 * (b - Q) + g
                            dve.tensor_tensor(rope_a[:, r_, :], ps[:, :], cosT[:, :], ALU.mult)
                            for to, frm in ((slice(0, 64), slice(64, P)), (slice(64, P), slice(0, 64))):
                                last = dve.tensor_tensor(rope_b[to, r_, :], ps[frm, :], sinT[frm, :],
                                                         ALU.mult)
                            last.then_inc(evacuated[bank], 1)
                        if b == B:
                            dve.wait_ge(taps, 3 * (2 * c + g) + 3)
                            dve.tensor_tensor(z[:, g, :], ps[:, :], conv[:, g, :],
                                              ALU.mult).then_inc(evacuated[bank], 1)
                    if b == GC:
                        for g in range(2):
                            dve.wait_ge(z_hi_ready, 2 * c + g + 1)
                            dve.tensor_tensor(zh_lo[:, bass.ds(2 * c + g, 1), :], z[:, g, :],
                                              as_f32(zh_hi[:, bass.ds(2 * c + g, 1), :]),
                                              ALU.subtract).then_inc(z_lo_ready, 1)
                    if b == GA:
                        dve.wait_ge(attn_hi_ready, c + 1)
                        dve.tensor_tensor(attn_lo[:, bass.ds(2 * c, 2), :], wide[:, 0, :],
                                          as_f32(attn_hi[:, bass.ds(2 * c, 2), :]),
                                          ALU.subtract).then_inc(attn_lo_ready, 1)

            with dve.Fori(0, 2) as i:
                for q in range(4):
                    n = N_D + 4 * i + q
                    split_lo((q + 2) % RING, n + 2)
                    side, gate = (gated_a, gate_a) if q % 2 else (gated_c, gate_c)
                    for g in range(2):
                        bank = 2 * (q % 2) + g
                        dve.wait_ge(*((left_done, left(n)) if g == 0 else (block_done, done(n))))
                        at = q - q % 2 + g
                        dve.scalar_tensor_tensor(out=side[:, at, :], in0=gate[:, bass.ds(4 * i + at, 1), :],
                                                 scalar=1.0, in1=ring_ps[bank][:, :], op0=ALU.add,
                                                 op1=ALU.mult).then_inc(evacuated[bank], 1)
                    if q % 2:
                        for g in range(2):
                            j = 4 * i + q - 1 + g
                            dve.wait_ge(m_hi_ready, j + 1)
                            dve.scalar_tensor_tensor(out=xm_lo[:, bass.ds(j, 1), :],
                                                     in0=merged[:, q - 1 + g, :], scalar=0.5,
                                                     in1=as_f32(xm_hi[:, bass.ds(j, 1), :]), op0=ALU.mult,
                                                     op1=ALU.subtract).then_inc(m_lo_ready, 1)
            for q in range(4):
                split_lo((q + 2) % RING if q < 2 else q - 2, N_E + q + 2)
                for g in range(2):
                    j = 2 * q + g
                    bank = j % BANKS
                    dve.wait_ge(h_hi_ready, j + 1)
                    dve.scalar_tensor_tensor(out=zh_lo[:, j, :], in0=ring_ps[bank][:, :],
                                             scalar=consts[:, ROW_GFFN + j:ROW_GFFN + j + 1],
                                             in1=as_f32(zh_hi[:, j, :]), op0=ALU.mult,
                                             op1=ALU.subtract).then_inc(evacuated[bank], 1)

            dve.wait_ge(stats_done, 1)
            dve.tensor_scalar(means[:, 2:4], wide[:, 3, 0:TT], 1.0 / D, EPS, ALU.mult,
                              ALU.add).then_inc(means_ready, 1)
            dve.wait_ge(rstd_ready, 2)
            for t in range(TT):
                dve.tensor_scalar(diag[:, t, :], ident[:, :], rstd[:, 2 + t:3 + t], None,
                                  ALU.mult).then_inc(diag_ready, 1)
            split_lo(2, N_F + 2)
            dve.wait_ge(bcast_done, 1)
            dve.tensor_copy(rstd_b[:, :], wide[:, 2, 0:S]).then_inc(rstd_b_ready, 1)
            dve.wait_ge(rstd_b_ready, 1)

            def side_done(k, p, g):
                n_left = N_F + 2 * p + k
                n = N_F + k if isinstance(p, int) and p == 0 else N_F + 3 * p - 1 + k
                dve.wait_ge(*((left_done, left(n_left)) if g == 0 else (block_done, done(n))))

            def take_up(p, par):
                for g in range(2):
                    side_done(0, p, g)
                    dve.tensor_tensor(up[:, 2 * par + g, :], ring_ps[g][:, :], rstd_b[:, :],
                                      ALU.mult).then_inc(evacuated[g], 1)

            def take_gate(p, par):
                for g in range(2):
                    side_done(1, p, g)
                    dve.tensor_tensor(fg[:, g, 2:S + 2], ring_ps[2 + g][:, :], rstd_b[:, :],
                                      ALU.mult).then_inc(evacuated[2 + g], 1)
                for i in (1, 0):
                    for g in range(2):
                        f = 2 * p + g
                        if i == 1:
                            dve.wait_ge(ftap, f + 1)
                        else:
                            dve.wait_ge(ftaps_dve, 4 * p + g + 1)
                        dve.scalar_tensor_tensor(out=fconv[:, 2 * par + g, :], in0=fg[:, g, i:S + i],
                                                 scalar=consts[:, bass.ds(ROW_FCONV + NF * i + f, 1)],
                                                 in1=fconv[:, 2 * par + g, :], op0=ALU.mult,
                                                 op1=ALU.add).then_inc(ftaps_dve, 1)

            def act_lo(p, par):
                for g in range(2):
                    dve.wait_ge(a_hi_ready, 2 * p + g + 1)
                    dve.tensor_tensor(ffn_lo[:, 2 * par + g, :], act[:, g, :], as_f32(ffn_hi[:, 2 * par + g, :]),
                                      ALU.subtract).then_inc(a_lo_ready, 1)

            take_up(0, 0)
            split_lo(0, N_F + 3)
            take_gate(0, 0)
            act_lo(0, 0)

            def pair(p, par, more=True):
                split_lo(1, N_F + 3 * p + 1)
                take_up(p, par)
                split_lo(2, N_F + 3 * p + 2)
                take_gate(p, par)
                if more:
                    split_lo(0, N_F + 3 * p + 3)
                act_lo(p, par)

            with dve.Fori(0, NP // 2 - 1) as i:
                pair(2 * i + 1, 1)
                pair(2 * i + 2, 0)
            pair(NP - 2, 1)
            pair(NP - 1, 0, more=False)

            dve.wait_ge(g_final_loaded, 16)
            for t in range(TT):
                for half in range(2):
                    i = 2 * t + half
                    dve.wait_ge(sums_ready, TT + i + 1)
                    at = slice(512 * half, 512 * (half + 1))
                    dve.tensor_tensor(scratch[:, t, at], wide[:, i, :], g_final[:, at],
                                      ALU.mult).then_inc(gained, 1)
                dve.wait_ge(rstd_ready, 3 + t)
                dve.wait_ge(gained, 2 * t + 2)
                dve.tensor_scalar(scratch[:, t, 512:D], scratch[:, t, 512:D], rstd[:, 4 + t:5 + t], None,
                                  ALU.mult).then_inc(right_out_ready, 1)

        @block.tensor
        def _(pe):
            def transpose(to, frm, start=True, stop=True):
                return pe.matmul(to, frm, ident[:, :], start=start, stop=stop, is_transpose=True,
                                 skip_group_check=True)

            def arrived(n):
                pe.wait_ge(lo_ready, n + 1)

            def project(n, bank_at, use, slot, hi, lo, seed=None, before=None, between=None, left_only=None):
                if left_only is None:
                    arrived(n)
                whi = w_hi[slot][:, :].rearrange("p (k c) -> p k c", k=KD)
                wlo = w_lo[slot][:, :].rearrange("p (k c) -> p k c", k=KD)
                for g in range(2):
                    bank = (bank_at + g) % BANKS
                    if g and left_only is not None:
                        arrived(n)
                    pe.wait_ge(evacuated[bank], free_for(use))
                    to = ring_ps[bank][:, :]
                    if seed:
                        seed(g, ring_ps[bank])
                    cols = slice(P * g, P * (g + 1))
                    passes = ((whi, hi), (whi, lo), (wlo, hi))
                    order = ([(k, i) for i in range(3) for k in range(KD)] if left_only is not None
                             else [(k, i) for k in range(KD) for i in range(3)])
                    for at, (k, i) in enumerate(order):
                        if before and g == 0:
                            before(k, i)
                        w, a = passes[i]
                        last = pe.matmul(to, w[:, k, cols], a[:, k, :], start=(at == 0 and not seed),
                                         stop=(at == len(order) - 1), skip_group_check=True)
                    last.then_inc(left_done if g == 0 else block_done, 1)
                    if between and g == 0:
                        between()

            pe.sem_inc(block_done, RING)
            for bank in range(BANKS):
                pe.sem_inc(evacuated[bank], 1)

            pe.wait_ge(setup, 9)
            pe.wait_ge(rows_loaded, 5 * 16)
            transpose(ring_ps[3][:, 0:P], consts_rows[:, :]).then_inc(consts_seen, 1)
            for t in range(TT):
                pe.wait_ge(xn1_ready if t else xn0_ready, 1)
                for k in range(KD):
                    at = S * (k % 2) + P * t
                    last = transpose(wide[:, k // 2, at:at + P], xn_tok[:, t, P * k:P * (k + 1)])
            last.then_inc(xT_done, 1)
            pe.wait_ge(consts_ready, 1)

            with pe.Fori(0, STEPS) as c:
                for b in range(PER_STEP):
                    n, use = PER_STEP * c + b, 4 * c + 2 * b // BANKS
                    slot, bank_at = b % RING, 2 * b % BANKS
                    if b == V:
                        arrived(n)
                        whi = w_hi[slot][:, :].rearrange("p (k c) -> p k c", k=KD)
                        wlo = w_lo[slot][:, :].rearrange("p (k c) -> p k c", k=KD)
                        for g in range(2):
                            bank = bank_at + g
                            pe.wait_ge(evacuated[bank], free_for(use))
                            for k in range(KD):
                                toks = slice(P * g, P * (g + 1))
                                for i, (a, w) in enumerate(((xm_hi, whi), (xm_lo, whi), (xm_hi, wlo))):
                                    last = pe.matmul(ring_ps[bank][:, :], a[:, k, toks], w[:, k, :],
                                                     start=(k == 0 and i == 0),
                                                     stop=(k == KD - 1 and i == 2))
                            last.then_inc(left_done if g == 0 else block_done, 1)
                        pe.wait_ge(rope_added, 4 * c + 4)
                        for h in range(2):
                            pe.matmul(wide[:, h, 0:P], qkT[:, h, 0:P], qkT[:, 2 + h, 0:P],
                                      start=True, stop=True)
                            pe.matmul(wide[:, h, P:3 * P], qkT[:, h, P:S], qkT[:, 2 + h, :],
                                      start=True, stop=True).then_inc(scores_done, 1)
                    elif b == X:
                        def parts_there(k, i):
                            if i == 0 and k == 0:
                                pe.wait_ge(left_hi_ready, c + 1)
                            if i < 2:
                                pe.wait_ge((x_hi_ready, x_lo_ready)[i], k + 1)
                            elif k == 0:
                                pe.wait_ge(left_lo_ready, c + 1)

                        project(n, bank_at, use, slot, xm_hi, xm_lo, left_only=c + 1,
                                before=parts_there)
                    elif b == GA:
                        def attend():
                            for h in range(2):
                                pe.wait_ge(probsT_ready, 2 * c + h + 1)
                                cols = slice(HD * h, HD * (h + 1))
                                pe.matmul(wide[:, 0, S * h:S * (h + 1)], v_tok[:, 0, cols],
                                          probsT[:, h, 0:2 * P], start=True, stop=False,
                                          skip_group_check=True)
                                last = pe.matmul(wide[:, 0, S * h + P:S * (h + 1)], v_tok[:, 1, cols],
                                                 probsT[:, h, 2 * P:3 * P], start=False, stop=True,
                                                 skip_group_check=True)
                            last.then_inc(attn_done, 1)

                        project(n, bank_at, use, slot, xm_hi, xm_lo, between=attend)
                    else:
                        project(n, bank_at, use, slot, xm_hi, xm_lo)
                    if b == GC:
                        pe.wait_ge(probs_ready, 4 * c + 4)
                        for h in range(2):
                            for i in range(3):
                                at = slice(P * i, P * (i + 1))
                                last = transpose(wide[:, 2 + h, at], probs_n[:, h, at])
                            last.then_inc(probsT_done, 1)

            pe.wait_ge(z_lo_ready, KD)
            with pe.Fori(0, 2) as i:
                for q in range(4):
                    hi, lo = (attn_hi, attn_lo) if q % 2 else (zh_hi, zh_lo)
                    if q == 1:
                        pe.wait_ge(attn_lo_ready, STEPS)
                    project(N_D + 4 * i + q, 2 * (q % 2), N_D * 2 // BANKS + 2 * i + q // 2, q, hi, lo)

            def m_ready(k, i):
                if i == 0:
                    pe.wait_ge(m_lo_ready, k + 1)

            for q in range(4):
                def residual(g, ps, q=q):
                    j = 2 * q + g
                    for t in range(TT):
                        transpose(ps[:, P * t:P * (t + 1)], x_tok[:, t, P * j:P * (j + 1)],
                                  start=(t == 0), stop=False)
                project(N_E + q, 2 * (q % 2), N_E * 2 // BANKS + q // 2, q, xm_hi, xm_lo, seed=residual,
                        before=m_ready if q == 0 else None)

            def h_ready(k, i):
                if i == 0:
                    pe.wait_ge(evacuated[k % BANKS], read_out(N_E * 2 // BANKS + k // BANKS))

            def statistics():
                pe.wait_ge(sumsq_ready, KD - 1)
                for t in range(TT):
                    last = pe.matmul(wide[:, 3, t:t + 1], sumsq[:, KD % 2, P * t:P * (t + 1)], ones[:, 0:1],
                                     start=True, stop=True, skip_group_check=True)
                last.then_inc(stats_done, 1)

            def broadcast():
                pe.wait_ge(diag_ready, TT)
                pe.matmul(wide[:, 2, 0:S], ones[:, :], diag[:, :, :], start=True,
                          stop=True).then_inc(bcast_done, 1)

            project(N_F, 0, USES_F, 0, zh_hi, zh_lo, before=h_ready, between=statistics)
            project(N_F + 1, 2, USES_F, 1, zh_hi, zh_lo, between=broadcast)
            pe.wait_ge(h_hi_ready, KD)
            pe.wait_ge(rstd_b_ready, 1)
            for t in range(TT):
                for k in range(KD):
                    transpose(wide[:, 2 * t + k // 4, P * (k % 4):P * (k % 4 + 1)],
                              hT[:, k, P * t:P * (t + 1)], start=(k % 4 == 0), stop=False)

            def down(n, p, par, slot, final=False):
                arrived(n)
                pe.wait_ge(a_lo_ready, 2 * p + 2)
                whi = w_hi[slot][:, :].rearrange("p (g c) -> p g c", g=2)
                wlo = w_lo[slot][:, :].rearrange("p (g c) -> p g c", g=2)
                for t in range(TT):
                    toks = slice(P * t, P * (t + 1))
                    passes = [(g, a, w) for g in range(2)
                              for a, w in ((ffn_hi, whi), (ffn_lo, whi), (ffn_hi, wlo))]
                    order = ([(q, half) for half in range(2) for q in passes] if final
                             else [(q, half) for q in passes for half in range(2)])
                    for at, ((g, a, w), half) in enumerate(order):
                        last_of_half = final and at % len(passes) == len(passes) - 1
                        last = pe.matmul(wide[:, 2 * t + half, :], a[:, 2 * par + g, toks],
                                         w[:, g, 512 * half:512 * (half + 1)], start=False,
                                         stop=last_of_half, skip_group_check=True)
                        if last_of_half:
                            last.then_inc(final_done, 1)
                if not final:
                    last.then_inc(block_done, 1)

            def pair(p, par):
                project(N_F + 3 * p - 1, 0, USES_F + p, 2, zh_hi, zh_lo)
                project(N_F + 3 * p, 2, USES_F + p, 0, zh_hi, zh_lo)
                down(N_F + 3 * p + 1, p - 1, 1 - par, 1)

            with pe.Fori(0, NP // 2) as i:
                pair(2 * i + 1, 1)
                pair(2 * i + 2, 0)
            down(N_F + 3 * NP - 1, NP - 1, 0, 2, final=True)


_INS = ["x", "positions", "norm_mix_g", "w_in", "conv_w", "w_conv_out", "w_attn_out", "w_out", "norm_ffn_g",
        "w_ffn_in", "ffn_conv_w", "ffn_conv_b", "w_ffn_down", "norm_final_g"]


def kernel(**inputs):
    import concourse.bacc as bacc
    from concourse.bass_utils import run_bass_kernel_spmd

    nc = bacc.Bacc("TRN2", target_bir_lowering=False, num_devices=1)
    arrays = {f"in_{name}": np.ascontiguousarray(inputs[name]) for name in _INS}
    half = np.exp(np.float32(-math.log(10000.0)) * np.arange(HD // 2, dtype=np.float32) * np.float32(2.0 / HD))
    cols = np.stack([np.tile(half, 2), np.repeat([1.0, -1.0], HD // 2), np.full(HD, math.pi / 2)], axis=1)
    arrays["in_rope_cols"] = np.ascontiguousarray(cols.astype(np.float32))
    args = [nc.dram_tensor(n, a.shape, mybir.dt.from_np(a.dtype), kind="ExternalInput").ap()
            for n, a in arrays.items()]
    out = nc.dram_tensor("out", (1, S, D), F32, kind="ExternalOutput").ap()
    layer(nc, *args, out)
    result = run_bass_kernel_spmd(nc, [arrays], core_ids=[0])
    return result.results[0]["out"]
```

```python
import math
from contextlib import ExitStack

import numpy as np
import concourse.bass as bass
from concourse import mybir

F32 = mybir.dt.float32
F32R = mybir.dt.float32r
I32 = mybir.dt.int32
ALU = mybir.AluOpType
ACT = mybir.ActivationFunctionType

P = 128
D = 1024
S = 256
TT = S // P
KD = D // P
HD = 128
DFF = 2816
NF = DFF // P
NP = NF // 2
BLK = 2048
COLS = BLK // KD
EPS = 1e-6
SCALE = HD ** -0.5
NEG = -1e30
RING = 4
RING_F = 3
BANKS = 4
STEPS = 4
PER_STEP = 8
N_D = STEPS * PER_STEP
N_E = N_D + 8
N_F = N_E + 4
USES_F = 2 * N_F // BANKS

X, C, Q, K, V, B, GC, GA = range(PER_STEP)
W_IN_PART = {X: 2, C: 1, Q: 3, K: 4, V: 5, B: 0, GC: 6, GA: 7}

ROW_CONV = 0
ROW_FCONV = ROW_CONV + 3 * KD
ROW_FBIAS = ROW_FCONV + 3 * NF
ROW_GMIX = ROW_FBIAS + NF
ROW_GFFN = ROW_GMIX + KD
assert ROW_GFFN + KD == P

ROUND = 1.5 * 2.0 ** 23
PI_IN = 3.1415925
ANGLE_STEPS = 18


def cut(value, bits, parts):
    out = []
    for _ in range(parts):
        e = math.floor(math.log2(abs(value))) - bits + 1
        out.append(math.floor(value / 2.0 ** e) * 2.0 ** e)
        value -= out[-1]
    return out + [float(np.float32(value))]


def layer(nc, x, positions, norm_mix_g, w_in, conv_w, w_conv_out, w_attn_out, w_out, norm_ffn_g,
          w_ffn_in, ffn_conv_w, ffn_conv_b, w_ffn_down, norm_final_g, rope_cols, out):
    rows = lambda w: w[0].rearrange("(k p) n -> p k n", p=P)
    w_in_v, w_conv_out_v, w_attn_out_v, w_out_v, w_ffn_in_v, w_ffn_down_v = map(
        rows, (w_in, w_conv_out, w_attn_out, w_out, w_ffn_in, w_ffn_down))
    x_v = x[0].rearrange("(t p) d -> p t d", p=P)
    out_v = out[0].rearrange("(t p) d -> p t d", p=P)

    ctx = ExitStack()
    with ctx:
        sb = lambda name, shape, dt=F32: ctx.enter_context(nc.sbuf_tensor(name, shape, dt))
        sem = lambda name: ctx.enter_context(nc.semaphore(name))

        raw = [sb(f"raw{i}", [P, BLK]) for i in range(RING)]
        w_hi = [sb(f"w_hi{i}", [P, BLK], F32R) for i in range(RING)]
        w_lo = [sb(f"w_lo{i}", [P, BLK], F32R) for i in range(RING)]
        xm_hi, xm_lo = sb("xm_hi", [P, KD, S], F32R), sb("xm_lo", [P, KD, S], F32R)
        zh_hi, zh_lo = sb("zh_hi", [P, KD, S], F32R), sb("zh_lo", [P, KD, S], F32R)
        attn_hi, attn_lo = sb("attn_hi", [P, KD, S], F32R), sb("attn_lo", [P, KD, S], F32R)
        ffn_hi, ffn_lo = attn_hi, attn_lo
        xT = sb("xT", [P, KD, S])
        scratch = sb("scratch", [P, TT, D])
        gate_c, gate_a = sb("gate_c", [P, KD, S]), sb("gate_a", [P, KD, S])
        hT = gate_c
        x_tok = gate_c[:, :, :].rearrange("p (t j) s -> p t (j s)", t=TT)
        consts_rows = sb("consts_rows", [P, P])
        consts = sb("consts", [P, P])
        ident, ones = sb("ident", [P, P]), sb("ones", [P, P])
        mask = sb("mask", [P, 3 * P])
        cosT, sinT = sb("cosT", [P, S]), sb("sinT", [P, S])
        rope_c = sb("rope_c", [P, 3])
        xs = sb("xs", [P, 2, S])
        cx = sb("cx", [P, 2, S + 2])
        conv = sb("conv", [P, 2, S])
        z = conv
        rope_a, rope_b = sb("rope_a", [P, 4, S]), sb("rope_b", [P, 4, S])
        qkT = sb("qkT", [P, 4, S])
        v_tok = sb("v_tok", [P, TT, 2 * HD])
        flat = scratch[:, :, :].rearrange("p t d -> p (t d)")
        masked = flat[:, 0:6 * P].rearrange("p (h s) -> p h s", h=2)
        probs = flat[:, 6 * P:12 * P].rearrange("p (h s) -> p h s", h=2)
        probs_n = masked
        rb = flat[:, 12 * P:12 * P + S]
        rb2 = flat[:, 12 * P + S:12 * P + 2 * S]
        probsT = sb("probsT", [P, 2, 3 * P])
        row_max, neg_max = sb("row_max", [P, 4]), sb("neg_max", [P, 4])
        row_sum, row_inv = sb("row_sum", [P, 4]), sb("row_inv", [P, 4])
        gated_c, gated_a = rope_a, rope_b
        merged = qkT
        up, silu = rope_a, rope_b
        fg = sb("fg", [P, 2, S + 2])
        fconv = qkT
        act = z
        sumsq = xs
        spare = gate_a[:, :, :].rearrange("p j s -> p (j s)")
        g_final = spare[:, 0:D]
        diag = spare[:, D:D + S].rearrange("p (t s) -> p t s", t=TT)
        rstd_b = spare[:, D + S:D + 2 * S]
        sums = sb("sums", [P, 8])
        means = sb("means", [P, 8])
        rstd = sb("rstd", [P, 8])
        minus_half = sb("minus_half", [P, 2])
        pos_i = rope_a[:, 0, :].bitcast(I32)
        angle = gate_a
        diag_in = gate_a[:, 5, :].rearrange("p (t s) -> p t s", t=TT)

        ring_ps = [ctx.enter_context(nc.psum_tensor(f"ring_ps{i}", [P, 2 * S], F32))[:, 0:S]
                   for i in range(BANKS)]
        wide = ctx.enter_context(nc.psum_tensor("wide", [P, 4, 512], F32))

        x_loaded = [sem(f"x_loaded{t}") for t in range(TT)]
        rows_loaded = sem("rows_loaded")
        rope_loaded = sem("rope_loaded")
        g_final_loaded = sem("g_final_loaded")
        half_loaded = sem("half_loaded")
        raw_loaded = [sem(f"raw_loaded{i}") for i in range(RING)]
        half_split = sem("half_split")
        hi_ready = sem("hi_ready")
        lo_ready = sem("lo_ready")
        slots_seen = sem("slots_seen")
        first_input = sem("first_input")
        left_lo_ready = sem("left_lo_ready")
        right_lo_ready = sem("right_lo_ready")
        left_done = sem("left_done")
        block_done = sem("block_done")
        evacuated = [sem(f"evacuated{i}") for i in range(BANKS)]
        setup = sem("setup")
        pool_steps = sem("pool_steps")
        sums_ready = sem("sums_ready")
        means_ready = sem("means_ready")
        rstd_ready = sem("rstd_ready")
        xs_scaled = sem("xs_scaled")
        conv_scaled = sem("conv_scaled")
        tables_scaled = sem("tables_scaled")
        rb2_ready = sem("rb2_ready")
        xT_ready = sem("xT_ready")
        gate_ready = sem("gate_ready")
        consts_seen = sem("consts_seen")
        consts_ready = sem("consts_ready")
        xT_done = sem("xT_done")
        x_hi_ready, x_lo_ready = sem("x_hi_ready"), sem("x_lo_ready")
        angles = sem("angles")
        tables_ready = sem("tables_ready")
        taps = sem("taps")
        z_hi_ready, z_lo_ready = sem("z_hi_ready"), sem("z_lo_ready")
        rope_added = sem("rope_added")
        scores_done, masked_done = sem("scores_done"), sem("masked_done")
        neg_max_ready, exp_done = sem("neg_max_ready"), sem("exp_done")
        inv_ready, probs_ready = sem("inv_ready"), sem("probs_ready")
        probsT_done, probsT_ready = sem("probsT_done"), sem("probsT_ready")
        attn_done = sem("attn_done")
        attn_hi_ready, attn_lo_ready = sem("attn_hi_ready"), sem("attn_lo_ready")
        merged_ready = sem("merged_ready")
        m_hi_ready, m_lo_ready = sem("m_hi_ready"), sem("m_lo_ready")
        squares_ready, sumsq_ready = sem("squares_ready"), sem("sumsq_ready")
        h_hi_ready, h_lo_ready = sem("h_hi_ready"), sem("h_lo_ready")
        stats_done, diag_ready, bcast_done = sem("stats_done"), sem("diag_ready"), sem("bcast_done")
        rstd_b_ready = sem("rstd_b_ready")
        ftap, ftaps_dve = sem("ftap"), sem("ftaps_dve")
        silu_ready, act_ready = sem("silu_ready"), sem("act_ready")
        a_hi_ready, a_lo_ready = sem("a_hi_ready"), sem("a_lo_ready")
        final_done = sem("final_done")
        half_mean = sem("half_mean")
        gained = sem("gained")
        left_out_ready, right_out_ready = sem("left_out_ready"), sem("right_out_ready")
        out_stored = sem("out_stored")

        left = lambda n: n + 1
        done = lambda n: n + 1 + RING
        slot_free = lambda n: done(n - RING)
        free_for = lambda k: k + 1
        read_out = lambda k: k + 2

        as_f32 = lambda ap: ap.bitcast(F32)

        def lo_side(engine, slot, side, signal):
            at = lambda w: w[slot][:, :].rearrange("p (k c) -> p k c", k=KD)[:, :, P * side:P * (side + 1)]
            engine.tensor_tensor(at(w_lo), at(raw), as_f32(at(w_hi)), ALU.subtract).then_inc(signal, 1)

        block = ctx.enter_context(nc.Block())

        @block.sync
        def _(sp):
            def load(slot, use, n, source):
                if n is not None:
                    sp.wait_ge(lo_ready, n - RING + 1)
                    sp.sem_inc(slots_seen, 1)
                sp.dma_start(raw[slot][:, :].rearrange("p (k c) -> p k c", k=source.shape[1]),
                             source).then_inc(raw_loaded[slot], 16)

            part = lambda b, c: w_in_v[:, :, bass.ds(W_IN_PART[b] * D + COLS * c, COLS)]
            for t in range(TT):
                sp.dma_start(x_tok[:, t, :], x_v[:, t, :]).then_inc(x_loaded[t], 16)
            at = 0
            for source in (conv_w[0].rearrange("i (j p) -> (i j) p", p=P),
                           ffn_conv_w[0].rearrange("i (j p) -> (i j) p", p=P),
                           ffn_conv_b[0].rearrange("(j p) -> j p", p=P),
                           norm_mix_g[0].rearrange("(j p) -> j p", p=P),
                           norm_ffn_g[0].rearrange("(j p) -> j p", p=P)):
                sp.dma_start(consts_rows[at:at + source.shape[0], :], source).then_inc(rows_loaded, 16)
                at += source.shape[0]
            half = KD // 2
            raw0 = raw[0][:, :].rearrange("p (k c) -> p k c", k=KD)
            sp.dma_start(raw0[:, 0:half, :], part(0, 0)[:, 0:half, :]).then_inc(half_loaded, 16)
            sp.dma_start(raw0[:, half:KD, :], part(0, 0)[:, half:KD, :]).then_inc(raw_loaded[0], 16)
            for b in range(1, RING):
                load(b, 0, None, part(b, 0))
            with sp.Fori(0, STEPS - 1) as c:
                for b in range(RING, PER_STEP):
                    load(b % RING, None, PER_STEP * c + b, part(b, c))
                for b in range(RING):
                    load(b, None, PER_STEP * c + b + PER_STEP, part(b, c + 1))
            for b in range(RING, PER_STEP):
                load(b % RING, None, PER_STEP * (STEPS - 1) + b, part(b, STEPS - 1))
            for j in range(4):
                for i, source in enumerate((w_conv_out_v, w_attn_out_v)):
                    n = N_D + 2 * j + i
                    load(n % RING, None, n, source[:, :, COLS * j:COLS * (j + 1)])
            for j in range(4):
                load(j, None, N_E + j, w_out_v[:, :, COLS * j:COLS * (j + 1)])

            def load_f(m, n_split, source):
                sp.wait_ge(lo_ready, n_split)
                sp.sem_inc(slots_seen, 1)
                sp.dma_start(raw[m][:, :].rearrange("p (k c) -> p k c", k=source.shape[1]),
                             source).then_inc(raw_loaded[m], 16)

            up_cols = lambda p: w_ffn_in_v[:, :, bass.ds(COLS * p, COLS)]
            gate_cols = lambda p: w_ffn_in_v[:, :, bass.ds(DFF + COLS * p, COLS)]
            down_rows = lambda p: w_ffn_down_v[:, bass.ds(2 * p, 2), :]
            load_f(0, N_F - 3, up_cols(0))
            load_f(1, N_F - 2, gate_cols(0))
            load_f(2, N_F - 1, up_cols(1))
            load_f(0, N_F + 1, gate_cols(1))
            load_f(1, N_F + 2, down_rows(0))
            with sp.Fori(2, NP) as p:
                load_f(2, N_F + 3 * p - 3, up_cols(p))
                load_f(0, N_F + 3 * p - 2, gate_cols(p))
                load_f(1, N_F + 3 * p - 1, down_rows(p - 1))
            load_f(2, N_F + 3 * NP - 3, down_rows(NP - 1))

            for i in range(2 * TT):
                t, half = divmod(i, 2)
                sp.wait_ge(right_out_ready if half else left_out_ready, t + 1)
                sp.dma_start(out_v[:, t, 512 * half:512 * (half + 1)],
                             scratch[:, t, 512 * half:512 * (half + 1)]).then_inc(out_stored, 16)
            sp.wait_ge(out_stored, 16 * 2 * TT)

        @block.gpsimd
        def _(pool):
            pool.memset(minus_half[:, :], -0.5).then_inc(setup, 1)
            pool.memset(ident[:, :], 0.0).then_inc(setup, 1)
            pool.wait_ge(setup, 2)
            pool.affine_select(out=ident[:, :], in_=ident[:, :], compare_op=ALU.not_equal, fill=1.0,
                               base=0, pattern=[[-1, P]], channel_multiplier=1).then_inc(setup, 1)
            pool.memset(mask[:, :], 0.0).then_inc(setup, 1)
            pool.memset(ones[:, :], 1.0).then_inc(setup, 1)
            pool.memset(cx[:, :, 0:2], 0.0).then_inc(setup, 1)
            pool.memset(fg[:, :, 0:2], 0.0).then_inc(setup, 1)
            pool.wait_ge(setup, 7)
            for tile, at in enumerate((slice(0, P), slice(P, 3 * P))):
                pool.affine_select(out=mask[:, at], in_=mask[:, at], compare_op=ALU.is_ge, fill=NEG,
                                   base=P * tile, pattern=[[-1, P * (tile + 1)]],
                                   channel_multiplier=1).then_inc(setup, 1)

            def inverse_root(at, mean_at, n=1):
                pool.tensor_tensor(rstd[:, at:at + n], means[:, mean_at:mean_at + n], minus_half[:, 0:n],
                                   ALU.pow).then_inc(rstd_ready, 1)

            for t in range(TT):
                pool.wait_ge(means_ready, t + 1)
                inverse_root(t, t)
            pool.wait_ge(hi_ready, 1)
            lo_side(pool, 0, 0, left_lo_ready)
            pool.wait_ge(right_lo_ready, 1)
            lo_side(pool, 1, 0, lo_ready)
            pool.wait_ge(evacuated[2], free_for(0))
            pool.tensor_tensor(rb2[:, :], rb[:, :], rb[:, :], ALU.mult).then_inc(rb2_ready, 1)
            pool.wait_ge(rb2_ready, 1)

            def scale_xs(c):
                for g in range(2):
                    pool.wait_ge(evacuated[g], read_out(4 * c))
                    pool.tensor_tensor(xs[:, g, :], xs[:, g, :], rb2[:, :],
                                       ALU.mult).then_inc(xs_scaled, 1)

            def rotate_and_scale_conv(c):
                for r in range(4):
                    bank, use = r % BANKS, 4 * c + 1
                    pool.wait_ge(evacuated[bank], read_out(use))
                    pool.tensor_tensor(qkT[:, r, :], rope_a[:, r, :], rope_b[:, r, :],
                                       ALU.add).then_inc(rope_added, 1)
                for g in range(2):
                    pool.wait_ge(taps, 6 * c + 5 + g)
                    pool.tensor_tensor(conv[:, g, :], conv[:, g, :], rb[:, :],
                                       ALU.mult).then_inc(conv_scaled, 1)

            scale_xs(0)
            for i, table in enumerate((sinT, cosT)):
                pool.wait_ge(tables_ready, i + 1)
                pool.tensor_tensor(table[:, :], table[:, :], rb[:, :], ALU.mult).then_inc(tables_scaled, 1)
            with pool.Fori(0, STEPS - 1) as c:
                rotate_and_scale_conv(c)
                scale_xs(c + 1)
            rotate_and_scale_conv(STEPS - 1)

            with pool.Fori(0, 2) as i:
                for u in range(2):
                    for g in range(2):
                        pool.wait_ge(evacuated[2 + g], read_out(2 * N_D // BANKS + 2 * i + u))
                        pool.tensor_tensor(merged[:, 2 * u + g, :], gated_c[:, 2 * u + g, :],
                                           gated_a[:, 2 * u + g, :], ALU.add).then_inc(merged_ready, 1)

            pool.wait_ge(m_lo_ready, KD)
            pool.dma_start(g_final[:, :], norm_final_g.rearrange("(a n) -> a n", a=1)
                           .to_broadcast([P, D])).then_inc(g_final_loaded, 16)

            squares = scratch[:, :, :].rearrange("p t (j s) -> p (t j) s", s=S)
            for j in range(1, KD):
                pool.wait_ge(squares_ready, j + 1)
                if j > 1:
                    pool.wait_ge(sumsq_ready, j - 1)
                before = squares[:, 0, :] if j == 1 else sumsq[:, j % 2, :]
                pool.tensor_tensor(sumsq[:, (j + 1) % 2, :], before, squares[:, j, :],
                                   ALU.add).then_inc(sumsq_ready, 1)
            pool.wait_ge(means_ready, 3)
            inverse_root(2, 2, TT)

            def times_up(p, par):
                for g in range(2):
                    pool.wait_ge(silu_ready, 2 * p + g + 1)
                    pool.tensor_tensor(act[:, g, :], silu[:, 2 * par + g, :], up[:, 2 * par + g, :],
                                       ALU.mult).then_inc(act_ready, 1)

            times_up(0, 0)
            with pool.Fori(0, NP // 2) as i:
                times_up(2 * i + 1, 1)
                times_up(2 * i + 2, 0)
            for t in range(TT):
                pool.wait_ge(means_ready, 4 + t)
                inverse_root(4 + t, 6 + t)

        @block.scalar
        def _(act_):
            copy = lambda out_, in_, **k: act_.activation(out_, in_, ACT.Copy, **k)

            def split_hi(slot, use, n, free):
                act_.wait_ge(raw_loaded[slot], 16 * (use + 1))
                act_.wait_ge(block_done, free)
                copy(w_hi[slot][:, :], raw[slot][:, :]).then_inc(hi_ready, 1)

            for to, frm in ((pos_i[:, :], positions.to_broadcast([P, S])), (rope_c[:, :], rope_cols)):
                act_.dma_start(to, frm).then_inc(rope_loaded, 16)
            act_.wait_ge(first_input, 1)
            act_.activation(sums[:, 7:8], sums[:, 6:7], ACT.Square)
            for t in range(TT):
                act_.wait_ge(x_loaded[t], 16)
                act_.activation(scratch[:, t, :], x_tok[:, t, :], ACT.Square,
                                accum_out=sums[:, t:t + 1]).then_inc(sums_ready, 1)
                act_.wait_ge(sums_ready, t + 1)
                copy(means[:, t:t + 1], sums[:, t:t + 1], scale=1.0 / D, bias=EPS).then_inc(means_ready, 1)
            act_.wait_ge(consts_seen, 1)
            copy(consts[:, :], ring_ps[3][:, 0:P]).then_inc(consts_ready, 1)
            act_.wait_ge(consts_ready, 1)
            for k in range(KD):
                if k % 2 == 0:
                    act_.wait_ge(xT_done, k // 2 + 1)
                copy(xm_hi[:, k, :], wide[:, k // 2, S * (k % 2):S * (k % 2 + 1)],
                     scale=consts[:, ROW_GMIX + k:ROW_GMIX + k + 1]).then_inc(x_hi_ready, 1)
            act_.wait_ge(hi_ready, 1)
            split_hi(1, 0, 1, slot_free(1))
            split_hi(2, 0, 2, slot_free(2))

            def split_ahead(b, c):
                ahead = b + 3
                n = PER_STEP * c + ahead
                if ahead == PER_STEP:
                    act_.wait_ge(raw_loaded[0], 16 * (2 * c + 3))
                    act_.wait_ge(block_done, slot_free(n))
                    for half, signal in enumerate((half_split, hi_ready)):
                        at = slice(BLK // 2 * half, BLK // 2 * (half + 1))
                        copy(w_hi[0][:, at], raw[0][:, at]).then_inc(signal, 1)
                else:
                    split_hi(ahead % RING, 2 * c + ahead // RING, n, slot_free(n))

            def probabilities(b, c):
                if b == GA:
                    for h in range(2):
                        act_.wait_ge(probsT_done, 2 * c + h + 1)
                        copy(probsT[:, h, :], wide[:, 2 + h, 0:3 * P]).then_inc(probsT_ready, 1)

            def take_block(b, c):
                n0 = PER_STEP * c
                for g in range(2):
                    bank = (2 * b + g) % BANKS
                    if b in (X, V):
                        act_.wait_ge(*((left_done, left(n0 + b)) if g == 0
                                       else (block_done, done(n0 + b))))
                    if b == X:
                        copy(xs[:, g, :], ring_ps[bank][:, :]).then_inc(evacuated[bank], 1)
                    if b == V:
                        copy(v_tok[:, g, :], ring_ps[bank][:, :],
                             scale=rstd[:, g:g + 1]).then_inc(evacuated[bank], 1)
                    if b in (GC, GA):
                        gate = (gate_c if b == GC else gate_a)[:, bass.ds(2 * c + g, 1), :]
                        act_.wait_ge(evacuated[bank], read_out(4 * c + (2 * b + g) // BANKS))
                        act_.activation(gate, gate, ACT.Tanh, scale=0.5).then_inc(gate_ready, 1)
                if b == B:
                    for h in range(2):
                        act_.wait_ge(neg_max_ready, c + 1)
                        for i, at in enumerate((slice(0, P), slice(P, 3 * P))):
                            col = 2 * h + i
                            act_.activation(probs[:, h, at], masked[:, h, at], ACT.Exp,
                                            bias=neg_max[:, col:col + 1], scale=SCALE,
                                            accum_out=row_sum[:, col:col + 1]).then_inc(exp_done, 1)
                    for g in range(2):
                        bank = (2 * b + g) % BANKS
                        act_.wait_ge(evacuated[bank], read_out(4 * c + (2 * b + g) // BANKS))
                        copy(zh_hi[:, bass.ds(2 * c + g, 1), :], z[:, g, :]).then_inc(z_hi_ready, 1)
                if b == GA:
                    act_.wait_ge(attn_done, c + 1)
                    copy(attn_hi[:, bass.ds(2 * c, 2), :], wide[:, 0, :]).then_inc(attn_hi_ready, 1)

            take_block(X, 0)
            for i in range(4):
                act_.wait_ge(x_lo_ready, 2 * i + 2)
                copy(xT[:, 2 * i:2 * i + 2, :], wide[:, i, :]).then_inc(xT_ready, 1)
            split_ahead(X, 0)
            act_.wait_ge(angles, ANGLE_STEPS)
            act_.activation(sinT[:, :], angle[:, 3, :], ACT.Sin,
                            scale=rope_c[:, 1:2]).then_inc(tables_ready, 1)
            act_.activation(cosT[:, :], angle[:, 4, :], ACT.Sin, scale=-1.0,
                            bias=rope_c[:, 2:3]).then_inc(tables_ready, 1)
            with act_.Fori(0, STEPS - 1) as c:
                for b in range(C, PER_STEP):
                    probabilities(b, c)
                    split_ahead(b, c)
                    take_block(b, c)
                split_ahead(X, c + 1)
                take_block(X, c + 1)
            for b in range(C, PER_STEP):
                probabilities(b, STEPS - 1)
                split_ahead(b, STEPS - 1)
                take_block(b, STEPS - 1)

            with act_.Fori(0, 2) as i:
                for q in range(4):
                    ahead = q + 3
                    n = N_D + 4 * i + ahead
                    split_hi(ahead % RING, N_D // RING + i + ahead // RING, n, slot_free(n))
                    if q % 2:
                        for g in range(2):
                            j = 4 * i + q - 1 + g
                            act_.wait_ge(merged_ready, j + 1)
                            copy(xm_hi[:, bass.ds(j, 1), :], merged[:, q - 1 + g, :],
                                 scale=0.5).then_inc(m_hi_ready, 1)
            squares = scratch[:, :, :].rearrange("p t (j s) -> p (t j) s", s=S)
            for q in range(4):
                n = N_E + q + 3
                if q < 1:
                    split_hi(q + 3, N_E // RING, n, slot_free(n))
                elif q < 3:
                    split_hi(q - 1, N_F // RING, n, slot_free(n))
                for g in range(2):
                    j = 2 * q + g
                    bank = j % BANKS
                    act_.wait_ge(evacuated[bank], read_out(N_E * 2 // BANKS + q // 2))
                    copy(zh_hi[:, j, :], hT[:, j, :],
                         scale=consts[:, ROW_GFFN + j:ROW_GFFN + j + 1]).then_inc(h_hi_ready, 1)
                    act_.activation(squares[:, j, :], hT[:, j, :], ACT.Square).then_inc(squares_ready, 1)

            def split_hi_f(m, n, use):
                act_.wait_ge(raw_loaded[m], 16 * (use + 1))
                act_.wait_ge(block_done, done(n - RING_F))
                copy(w_hi[m][:, :], raw[m][:, :]).then_inc(hi_ready, 1)

            first_f = N_F // RING

            def gate_conv(p, par):
                for g in range(2):
                    f = 2 * p + g
                    col = lambda row: consts[:, bass.ds(row + f, 1)]
                    act_.wait_ge(evacuated[2 + g], read_out(USES_F + p))
                    act_.activation(fconv[:, 2 * par + g, :], fg[:, g, 2:S + 2], ACT.Identity,
                                    scale=col(ROW_FCONV + 2 * NF), bias=col(ROW_FBIAS)).then_inc(ftap, 1)

            def gate_silu(p, par):
                for g in range(2):
                    act_.wait_ge(ftaps_dve, 4 * p + 3 + g)
                    act_.activation(silu[:, 2 * par + g, :], fconv[:, 2 * par + g, :],
                                    ACT.Silu).then_inc(silu_ready, 1)
                for g in range(2):
                    act_.wait_ge(act_ready, 2 * p + g + 1)
                    copy(ffn_hi[:, 2 * par + g, :], act[:, g, :]).then_inc(a_hi_ready, 1)

            split_hi_f(2, N_F + 2, first_f)
            split_hi_f(0, N_F + 3, first_f + 1)
            gate_conv(0, 0)
            gate_silu(0, 0)

            def pair(p, par):
                split_hi_f(1, N_F + 3 * p + 1, first_f + p)
                split_hi_f(2, N_F + 3 * p + 2, first_f + p)
                gate_conv(p, par)
                return N_F + 3 * p + 3

            with act_.Fori(0, NP // 2 - 1) as i:
                for u, par in ((1, 1), (2, 0)):
                    p = 2 * i + u
                    n = pair(p, par)
                    split_hi_f(0, n, first_f + p + 1)
                    gate_silu(p, par)
            n = pair(NP - 2, 1)
            split_hi_f(0, n, first_f + NP - 1)
            gate_silu(NP - 2, 1)
            pair(NP - 1, 0)
            gate_silu(NP - 1, 0)

            unused = gate_c[:, :, :].rearrange("p j s -> p (j s)")
            for t in range(TT):
                for half in range(2):
                    i = 2 * t + half
                    act_.wait_ge(final_done, i + 1)
                    act_.activation(unused[:, 512 * i:512 * (i + 1)], wide[:, i, :], ACT.Square,
                                    accum_out=sums[:, 4 + i:5 + i]).then_inc(sums_ready, 1)
                    act_.wait_ge(sums_ready, TT + i + 1)
                    if half == 0:
                        copy(means[:, 4 + t:5 + t], sums[:, 4 + i:5 + i], scale=1.0 / D,
                             bias=EPS).then_inc(half_mean, 1)
                    else:
                        act_.wait_ge(half_mean, t + 1)
                        act_.activation(means[:, 6 + t:7 + t], sums[:, 4 + i:5 + i], ACT.Identity,
                                        scale=1.0 / D, bias=means[:, 4 + t:5 + t]).then_inc(means_ready, 1)
                act_.wait_ge(rstd_ready, 4 + t)
                act_.wait_ge(gained, 2 * t + 1)
                copy(scratch[:, t, 0:512], scratch[:, t, 0:512],
                     scale=rstd[:, 4 + t:5 + t]).then_inc(left_out_ready, 1)

        @block.vector
        def _(dve):
            def split_lo(slot, n):
                dve.wait_ge(hi_ready, n + 1)
                dve.tensor_tensor(w_lo[slot][:, :], raw[slot][:, :], as_f32(w_hi[slot][:, :]),
                                  ALU.subtract).then_inc(lo_ready, 1)

            r, t_, a1, red, mag = (angle[:, i, :] for i in range(5))
            count = [0]

            def step(ins):
                ins.then_inc(angles, 1)
                count[0] += 1

            def after_last():
                dve.wait_ge(angles, count[0])

            dve.memset(sums[:, 6:7], 0.0).then_inc(first_input, 1)
            dve.wait_ge(rope_loaded, 32)
            step(dve.tensor_scalar(r, pos_i[:, :], rope_c[:, 0:1], None, ALU.mult))
            big = 2 * math.pi * 4096
            after_last()
            step(dve.tensor_scalar(t_, r, 1.0 / big, ROUND, ALU.mult, ALU.add))
            after_last()
            step(dve.tensor_scalar(t_, t_, -ROUND, None, ALU.add))
            after_last()
            step(dve.tensor_scalar(a1, t_, 64 * ROUND, -64 * ROUND, ALU.add, ALU.add))
            after_last()
            step(dve.tensor_tensor(t_, t_, a1, ALU.subtract))
            for t in range(TT):
                dve.wait_ge(rstd_ready, t + 1)
                dve.tensor_scalar(diag_in[:, t, :], ident[:, :], rstd[:, t:t + 1], None,
                                  ALU.mult).then_inc(diag_ready, 1)

            def split_half(half, after):
                at = slice(BLK // 2 * half, BLK // 2 * (half + 1))
                dve.tensor_copy(w_hi[0][:, at], raw[0][:, at]).then_inc(after, 1)

            dve.wait_ge(half_loaded, 16)
            split_half(0, half_split)
            dve.wait_ge(consts_ready, 1)
            for k in range(KD):
                if k == 2:
                    dve.wait_ge(raw_loaded[0], 16)
                    dve.wait_ge(half_split, 1)
                    split_half(1, hi_ready)
                dve.wait_ge(x_hi_ready, 2 * (k // 2) + 2)
                dve.scalar_tensor_tensor(out=xm_lo[:, k, :], in0=wide[:, k // 2, S * (k % 2):S * (k % 2 + 1)],
                                         scalar=consts[:, ROW_GMIX + k:ROW_GMIX + k + 1],
                                         in1=as_f32(xm_hi[:, k, :]), op0=ALU.mult,
                                         op1=ALU.subtract).then_inc(x_lo_ready, 1)
            dve.wait_ge(left_lo_ready, 1)
            dve.wait_ge(hi_ready, 1)
            lo_side(dve, 0, 1, lo_ready)
            dve.wait_ge(bcast_done, 1)
            dve.tensor_copy(rb[:, :], ring_ps[2][:, :]).then_inc(evacuated[2], 1)
            dve.wait_ge(hi_ready, 2)
            lo_side(dve, 1, 1, right_lo_ready)
            for const in cut(big, 12, 2):
                for turns in (a1, t_):
                    after_last()
                    step(dve.scalar_tensor_tensor(out=r, in0=turns, scalar=-const, in1=r,
                                                  op0=ALU.mult, op1=ALU.add))
            after_last()
            step(dve.tensor_scalar(t_, r, 1.0 / (2 * math.pi), ROUND, ALU.mult, ALU.add))
            after_last()
            step(dve.tensor_scalar(t_, t_, -ROUND, None, ALU.add))
            for const in cut(2 * math.pi, 12, 2):
                after_last()
                step(dve.scalar_tensor_tensor(out=r, in0=t_, scalar=-const, in1=r,
                                              op0=ALU.mult, op1=ALU.add))
            dve.wait_ge(lo_ready, 2)
            split_lo(2, 2)
            after_last()
            step(dve.tensor_scalar(red, r, PI_IN, -PI_IN, ALU.min, ALU.max))
            step(dve.scalar_tensor_tensor(out=mag, in0=r, scalar=-1.0, in1=r, op0=ALU.mult, op1=ALU.max))
            assert count[0] == ANGLE_STEPS
            dve.wait_ge(setup, 9)

            def after_block(b, c):
                n0 = PER_STEP * c
                def split_ahead():
                    if b + 2 == PER_STEP:
                        dve.wait_ge(hi_ready, n0 + b + 3)
                        lo_side(dve, 0, 0, left_lo_ready)
                        lo_side(dve, 0, 1, lo_ready)
                    else:
                        split_lo((b + 2) % RING, n0 + b + 2)

                if b != GC:
                    split_ahead()
                if b == B:
                    dve.wait_ge(scores_done, 2 * c + 2)
                    dve.tensor_tensor(masked[:, :, :], wide[:, 0:2, 0:3 * P],
                                      mask[:, None, :].to_broadcast([P, 2, 3 * P]),
                                      ALU.add).then_inc(masked_done, 1)
                    dve.wait_ge(masked_done, 3 * c + 1)
                    for i, at in enumerate((slice(0, P), slice(P, 3 * P))):
                        dve.reduce_max(row_max[:, i:i + 3:2], masked[:, :, at],
                                       mybir.AxisListType.X).then_inc(masked_done, 1)
                    dve.wait_ge(masked_done, 3 * c + 3)
                    dve.tensor_scalar(neg_max[:, :], row_max[:, :], -SCALE, None,
                                      ALU.mult).then_inc(neg_max_ready, 1)
                if b == GC:
                    dve.wait_ge(exp_done, 4 * c + 4)
                    dve.reciprocal(row_inv[:, :], row_sum[:, :]).then_inc(inv_ready, 1)
                    dve.wait_ge(inv_ready, c + 1)
                    for h in range(2):
                        for i, at in enumerate((slice(0, P), slice(P, 3 * P))):
                            col = 2 * h + i
                            dve.tensor_scalar(probs_n[:, h, at], probs[:, h, at],
                                              row_inv[:, col:col + 1], None,
                                              ALU.mult).then_inc(probs_ready, 1)
                    split_ahead()
                if b == Q:
                    dve.wait_ge(tables_scaled, 2)
                if b == V:
                    for i in (2, 1, 0):
                        for g in range(2):
                            tap = consts[:, bass.ds(ROW_CONV + KD * i + 2 * c + g, 1)]
                            if i == 2:
                                dve.wait_ge(evacuated[2 + g], read_out(4 * c))
                                dve.tensor_scalar(conv[:, g, :], cx[:, g, 2:S + 2], tap, None,
                                                  ALU.mult).then_inc(taps, 1)
                            else:
                                dve.wait_ge(taps, 6 * c + 2 * (1 - i) + g + 1)
                                dve.scalar_tensor_tensor(out=conv[:, g, :], in0=cx[:, g, i:S + i],
                                                         scalar=tap, in1=conv[:, g, :],
                                                         op0=ALU.mult, op1=ALU.add).then_inc(taps, 1)
                for g in range(2):
                    bank, use = (2 * b + g) % BANKS, 4 * c + (2 * b + g) // BANKS
                    ps = ring_ps[bank]
                    if b in (C, Q, K, B, GC, GA):
                        dve.wait_ge(*((left_done, left(n0 + b)) if g == 0
                                      else (block_done, done(n0 + b))))
                    if b == C:
                        dve.wait_ge(xs_scaled, 2 * c + g + 1)
                        dve.tensor_tensor(cx[:, g, 2:S + 2], ps[:, :], xs[:, g, :],
                                          ALU.mult).then_inc(evacuated[bank], 1)
                    if b in (Q, K):
                        r_ = 2 * (b - Q) + g
                        dve.tensor_tensor(rope_a[:, r_, :], ps[:, :], cosT[:, :], ALU.mult)
                        for to, frm in ((slice(0, 64), slice(64, P)), (slice(64, P), slice(0, 64))):
                            last = dve.tensor_tensor(rope_b[to, r_, :], ps[frm, :], sinT[frm, :],
                                                     ALU.mult)
                        last.then_inc(evacuated[bank], 1)
                    if b == B:
                        dve.wait_ge(conv_scaled, 2 * c + g + 1)
                        dve.tensor_tensor(z[:, g, :], ps[:, :], conv[:, g, :],
                                          ALU.mult).then_inc(evacuated[bank], 1)
                    if b in (GC, GA):
                        dve.tensor_tensor((gate_c if b == GC else gate_a)[:, bass.ds(2 * c + g, 1), :],
                                          ps[:, :], rb[:, :], ALU.mult).then_inc(evacuated[bank], 1)
                if b == GC:
                    for g in range(2):
                        dve.wait_ge(z_hi_ready, 2 * c + g + 1)
                        dve.tensor_tensor(zh_lo[:, bass.ds(2 * c + g, 1), :], z[:, g, :],
                                          as_f32(zh_hi[:, bass.ds(2 * c + g, 1), :]),
                                          ALU.subtract).then_inc(z_lo_ready, 1)
                if b == GA:
                    dve.wait_ge(attn_hi_ready, c + 1)
                    dve.tensor_tensor(attn_lo[:, bass.ds(2 * c, 2), :], wide[:, 0, :],
                                      as_f32(attn_hi[:, bass.ds(2 * c, 2), :]),
                                      ALU.subtract).then_inc(attn_lo_ready, 1)


            with dve.Fori(0, STEPS - 1) as c:
                for b in range(C, PER_STEP):
                    after_block(b, c)
                after_block(X, c + 1)
            for b in range(C, PER_STEP):
                after_block(b, STEPS - 1)

            dve.wait_ge(gate_ready, 4 * STEPS)
            with dve.Fori(0, 2) as i:
                for q in range(4):
                    n = N_D + 4 * i + q
                    split_lo((q + 2) % RING, n + 2)
                    side, gate = (gated_a, gate_a) if q % 2 else (gated_c, gate_c)
                    for g in range(2):
                        bank = 2 * (q % 2) + g
                        dve.wait_ge(*((left_done, left(n)) if g == 0 else (block_done, done(n))))
                        at = q - q % 2 + g
                        dve.scalar_tensor_tensor(out=side[:, at, :], in0=gate[:, bass.ds(4 * i + at, 1), :],
                                                 scalar=1.0, in1=ring_ps[bank][:, :], op0=ALU.add,
                                                 op1=ALU.mult).then_inc(evacuated[bank], 1)
                    if q % 2:
                        for g in range(2):
                            j = 4 * i + q - 1 + g
                            dve.wait_ge(m_hi_ready, j + 1)
                            dve.scalar_tensor_tensor(out=xm_lo[:, bass.ds(j, 1), :],
                                                     in0=merged[:, q - 1 + g, :], scalar=0.5,
                                                     in1=as_f32(xm_hi[:, bass.ds(j, 1), :]), op0=ALU.mult,
                                                     op1=ALU.subtract).then_inc(m_lo_ready, 1)
            for q in range(4):
                split_lo((q + 2) % RING if q < 2 else q - 2, N_E + q + 2)
                for g in range(2):
                    j = 2 * q + g
                    dve.wait_ge(*((left_done, left(N_E + q)) if g == 0 else (block_done, done(N_E + q))))
                    dve.tensor_tensor(hT[:, j, :], ring_ps[j % BANKS][:, :], xT[:, j, :],
                                      ALU.add).then_inc(evacuated[j % BANKS], 1)
                for g in range(2):
                    j = 2 * q + g
                    dve.wait_ge(h_hi_ready, j + 1)
                    dve.scalar_tensor_tensor(out=zh_lo[:, j, :], in0=hT[:, j, :],
                                             scalar=consts[:, ROW_GFFN + j:ROW_GFFN + j + 1],
                                             in1=as_f32(zh_hi[:, j, :]), op0=ALU.mult,
                                             op1=ALU.subtract).then_inc(h_lo_ready, 1)

            dve.wait_ge(stats_done, 1)
            dve.tensor_scalar(means[:, 2:4], wide[:, 3, 0:TT], 1.0 / D, EPS, ALU.mult,
                              ALU.add).then_inc(means_ready, 1)
            dve.wait_ge(rstd_ready, 3)
            for t in range(TT):
                dve.tensor_scalar(diag[:, t, :], ident[:, :], rstd[:, 2 + t:3 + t], None,
                                  ALU.mult).then_inc(diag_ready, 1)
            split_lo(2, N_F + 2)
            dve.wait_ge(bcast_done, 2)
            dve.tensor_copy(rstd_b[:, :], wide[:, 2, 0:S]).then_inc(rstd_b_ready, 1)
            dve.wait_ge(rstd_b_ready, 1)

            def side_done(k, p, g):
                n_left = N_F + 2 * p + k
                n = N_F + k if isinstance(p, int) and p == 0 else N_F + 3 * p - 1 + k
                dve.wait_ge(*((left_done, left(n_left)) if g == 0 else (block_done, done(n))))

            def take_up(p, par):
                for g in range(2):
                    side_done(0, p, g)
                    dve.tensor_tensor(up[:, 2 * par + g, :], ring_ps[g][:, :], rstd_b[:, :],
                                      ALU.mult).then_inc(evacuated[g], 1)

            def take_gate(p, par):
                for g in range(2):
                    side_done(1, p, g)
                    dve.tensor_tensor(fg[:, g, 2:S + 2], ring_ps[2 + g][:, :], rstd_b[:, :],
                                      ALU.mult).then_inc(evacuated[2 + g], 1)
                for i in (1, 0):
                    for g in range(2):
                        f = 2 * p + g
                        if i == 1:
                            dve.wait_ge(ftap, f + 1)
                        else:
                            dve.wait_ge(ftaps_dve, 4 * p + g + 1)
                        dve.scalar_tensor_tensor(out=fconv[:, 2 * par + g, :], in0=fg[:, g, i:S + i],
                                                 scalar=consts[:, bass.ds(ROW_FCONV + NF * i + f, 1)],
                                                 in1=fconv[:, 2 * par + g, :], op0=ALU.mult,
                                                 op1=ALU.add).then_inc(ftaps_dve, 1)

            def act_lo(p, par):
                for g in range(2):
                    dve.wait_ge(a_hi_ready, 2 * p + g + 1)
                    dve.tensor_tensor(ffn_lo[:, 2 * par + g, :], act[:, g, :], as_f32(ffn_hi[:, 2 * par + g, :]),
                                      ALU.subtract).then_inc(a_lo_ready, 1)

            take_up(0, 0)
            split_lo(0, N_F + 3)
            take_gate(0, 0)
            act_lo(0, 0)

            def pair(p, par, more=True):
                split_lo(1, N_F + 3 * p + 1)
                take_up(p, par)
                split_lo(2, N_F + 3 * p + 2)
                take_gate(p, par)
                if more:
                    split_lo(0, N_F + 3 * p + 3)
                act_lo(p, par)

            with dve.Fori(0, NP // 2 - 1) as i:
                pair(2 * i + 1, 1)
                pair(2 * i + 2, 0)
            pair(NP - 2, 1)
            pair(NP - 1, 0, more=False)

            dve.wait_ge(g_final_loaded, 16)
            for t in range(TT):
                for half in range(2):
                    i = 2 * t + half
                    dve.wait_ge(sums_ready, TT + i + 1)
                    at = slice(512 * half, 512 * (half + 1))
                    dve.tensor_tensor(scratch[:, t, at], wide[:, i, :], g_final[:, at],
                                      ALU.mult).then_inc(gained, 1)
                dve.wait_ge(rstd_ready, 4 + t)
                dve.wait_ge(gained, 2 * t + 2)
                dve.tensor_scalar(scratch[:, t, 512:D], scratch[:, t, 512:D], rstd[:, 4 + t:5 + t], None,
                                  ALU.mult).then_inc(right_out_ready, 1)

        @block.tensor
        def _(pe):
            def transpose(to, frm, start=True, stop=True):
                return pe.matmul(to, frm, ident[:, :], start=start, stop=stop, is_transpose=True,
                                 skip_group_check=True)

            def arrived(n):
                pe.wait_ge(lo_ready, n + 1)

            parts = lambda slot: [w[slot][:, :].rearrange("p (k c) -> p k c", k=KD) for w in (w_hi, w_lo)]

            def project(n, bank_at, use, slot, hi, lo, before=None, between=None):
                arrived(n)
                whi, wlo = parts(slot)
                for g in range(2):
                    bank = (bank_at + g) % BANKS
                    pe.wait_ge(evacuated[bank], free_for(use))
                    cols = slice(P * g, P * (g + 1))
                    for k in range(KD):
                        if before and g == 0:
                            before(k)
                        for i, (w, a) in enumerate(((whi, hi), (whi, lo), (wlo, hi))):
                            last = pe.matmul(ring_ps[bank][:, :], w[:, k, cols], a[:, k, :],
                                             start=(k == 0 and i == 0),
                                             stop=(k == KD - 1 and i == 2), skip_group_check=True)
                    last.then_inc(left_done if g == 0 else block_done, 1)
                    if between and g == 0:
                        between()

            def project_as_it_comes(n, bank_at, use, slot, first_hi, left_lo):
                whi, wlo = parts(slot)
                pe.wait_ge(*first_hi)
                for g in range(2):
                    pe.wait_ge(evacuated[bank_at + g], free_for(use))
                for i, (a, a_ready) in enumerate(((xm_hi, x_hi_ready), (xm_lo, x_lo_ready))):
                    for k in range(KD):
                        if i == 0 and k == KD // 2:
                            pe.wait_ge(hi_ready, n + 1)
                        pe.wait_ge(a_ready, k + 1)
                        for g in range(2):
                            pe.matmul(ring_ps[bank_at + g][:, :], whi[:, k, P * g:P * (g + 1)], a[:, k, :],
                                      start=(k == 0 and i == 0), stop=False, skip_group_check=True)
                for g in range(2):
                    pe.wait_ge(*((lo_ready, n + 1) if g else left_lo))
                    for k in range(KD):
                        last = pe.matmul(ring_ps[bank_at + g][:, :], wlo[:, k, P * g:P * (g + 1)],
                                         xm_hi[:, k, :], start=False, stop=(k == KD - 1),
                                         skip_group_check=True)
                    last.then_inc(block_done if g else left_done, 1)

            pe.sem_inc(block_done, RING)
            for bank in (0, 1, 3):
                pe.sem_inc(evacuated[bank], 1)

            pe.wait_ge(setup, 9)
            for t in range(TT):
                pe.wait_ge(x_loaded[t], 16)
                for k in range(KD):
                    if t and k == KD // 2:
                        pe.wait_ge(rows_loaded, 5 * 16)
                        transpose(ring_ps[3][:, 0:P], consts_rows[:, :]).then_inc(consts_seen, 1)
                    at = S * (k % 2) + P * t
                    last = transpose(wide[:, k // 2, at:at + P], x_tok[:, t, P * k:P * (k + 1)])
                    if t and k % 2:
                        last.then_inc(xT_done, 1)
            pe.wait_ge(diag_ready, TT)
            pe.matmul(ring_ps[2][:, :], ones[:, :], diag_in[:, :, :], start=True,
                      stop=True).then_inc(bcast_done, 1)
            pe.wait_ge(consts_ready, 1)

            with pe.Fori(0, STEPS) as c:
                for b in range(PER_STEP):
                    n, use = PER_STEP * c + b, 4 * c + 2 * b // BANKS
                    slot, bank_at = b % RING, 2 * b % BANKS
                    if b == V:
                        arrived(n)
                        whi, wlo = parts(slot)
                        for g in range(2):
                            bank = bank_at + g
                            pe.wait_ge(evacuated[bank], free_for(use))
                            for k in range(KD):
                                toks = slice(P * g, P * (g + 1))
                                for i, (a, w) in enumerate(((xm_hi, whi), (xm_lo, whi), (xm_hi, wlo))):
                                    last = pe.matmul(ring_ps[bank][:, :], a[:, k, toks], w[:, k, :],
                                                     start=(k == 0 and i == 0),
                                                     stop=(k == KD - 1 and i == 2))
                            last.then_inc(left_done if g == 0 else block_done, 1)
                        pe.wait_ge(rope_added, 4 * c + 4)
                        for h in range(2):
                            pe.matmul(wide[:, h, 0:P], qkT[:, h, 0:P], qkT[:, 2 + h, 0:P],
                                      start=True, stop=True)
                            pe.matmul(wide[:, h, P:3 * P], qkT[:, h, P:S], qkT[:, 2 + h, :],
                                      start=True, stop=True).then_inc(scores_done, 1)
                    elif b == X:
                        project_as_it_comes(n, bank_at, use, slot, (half_split, c + 1), (left_lo_ready, c + 1))
                    elif b in (C, Q):
                        project_as_it_comes(n, bank_at, use, slot, (hi_ready, n + 1), (lo_ready, n + 1))
                    elif b == GA:
                        def attend():
                            for h in range(2):
                                pe.wait_ge(probsT_ready, 2 * c + h + 1)
                                cols = slice(HD * h, HD * (h + 1))
                                pe.matmul(wide[:, 0, S * h:S * (h + 1)], v_tok[:, 0, cols],
                                          probsT[:, h, 0:2 * P], start=True, stop=False,
                                          skip_group_check=True)
                                last = pe.matmul(wide[:, 0, S * h + P:S * (h + 1)], v_tok[:, 1, cols],
                                                 probsT[:, h, 2 * P:3 * P], start=False, stop=True,
                                                 skip_group_check=True)
                            last.then_inc(attn_done, 1)

                        project(n, bank_at, use, slot, xm_hi, xm_lo, between=attend)
                    else:
                        project(n, bank_at, use, slot, xm_hi, xm_lo)
                    if b == GC:
                        pe.wait_ge(probs_ready, 4 * c + 4)
                        for h in range(2):
                            for i in range(3):
                                at = slice(P * i, P * (i + 1))
                                last = transpose(wide[:, 2 + h, at], probs_n[:, h, at])
                            last.then_inc(probsT_done, 1)

            pe.wait_ge(z_lo_ready, KD)
            with pe.Fori(0, 2) as i:
                for q in range(4):
                    hi, lo = (attn_hi, attn_lo) if q % 2 else (zh_hi, zh_lo)
                    if q == 1:
                        pe.wait_ge(attn_lo_ready, STEPS)
                    project(N_D + 4 * i + q, 2 * (q % 2), N_D * 2 // BANKS + 2 * i + q // 2, q, hi, lo)

            def m_ready(k):
                pe.wait_ge(m_lo_ready, k + 1)

            for q in range(4):
                project(N_E + q, 2 * (q % 2), N_E * 2 // BANKS + q // 2, q, xm_hi, xm_lo,
                        before=m_ready if q == 0 else None)

            def h_ready(k):
                pe.wait_ge(h_lo_ready, k + 1)

            def statistics():
                pe.wait_ge(sumsq_ready, KD - 1)
                for t in range(TT):
                    last = pe.matmul(wide[:, 3, t:t + 1], sumsq[:, KD % 2, P * t:P * (t + 1)], ones[:, 0:1],
                                     start=True, stop=True, skip_group_check=True)
                last.then_inc(stats_done, 1)

            def broadcast():
                pe.wait_ge(diag_ready, 2 * TT)
                pe.matmul(wide[:, 2, 0:S], ones[:, :], diag[:, :, :], start=True,
                          stop=True).then_inc(bcast_done, 1)

            project(N_F, 0, USES_F, 0, zh_hi, zh_lo, before=h_ready, between=statistics)
            project(N_F + 1, 2, USES_F, 1, zh_hi, zh_lo, between=broadcast)
            pe.wait_ge(h_hi_ready, KD)
            pe.wait_ge(rstd_b_ready, 1)
            for t in range(TT):
                for k in range(KD):
                    transpose(wide[:, 2 * t + k // 4, P * (k % 4):P * (k % 4 + 1)],
                              hT[:, k, P * t:P * (t + 1)], start=(k % 4 == 0), stop=False)

            def down(n, p, par, slot, final=False):
                arrived(n)
                pe.wait_ge(a_lo_ready, 2 * p + 2)
                whi = w_hi[slot][:, :].rearrange("p (g c) -> p g c", g=2)
                wlo = w_lo[slot][:, :].rearrange("p (g c) -> p g c", g=2)
                for t in range(TT):
                    toks = slice(P * t, P * (t + 1))
                    passes = [(g, a, w) for g in range(2)
                              for a, w in ((ffn_hi, whi), (ffn_lo, whi), (ffn_hi, wlo))]
                    order = ([(q, half) for half in range(2) for q in passes] if final
                             else [(q, half) for q in passes for half in range(2)])
                    for at, ((g, a, w), half) in enumerate(order):
                        last_of_half = final and at % len(passes) == len(passes) - 1
                        last = pe.matmul(wide[:, 2 * t + half, :], a[:, 2 * par + g, toks],
                                         w[:, g, 512 * half:512 * (half + 1)], start=False,
                                         stop=last_of_half, skip_group_check=True)
                        if last_of_half:
                            last.then_inc(final_done, 1)
                if not final:
                    last.then_inc(block_done, 1)

            def pair(p, par):
                project(N_F + 3 * p - 1, 0, USES_F + p, 2, zh_hi, zh_lo)
                project(N_F + 3 * p, 2, USES_F + p, 0, zh_hi, zh_lo)
                down(N_F + 3 * p + 1, p - 1, 1 - par, 1)

            with pe.Fori(0, NP // 2) as i:
                pair(2 * i + 1, 1)
                pair(2 * i + 2, 0)
            down(N_F + 3 * NP - 1, NP - 1, 0, 2, final=True)


_INS = ["x", "positions", "norm_mix_g", "w_in", "conv_w", "w_conv_out", "w_attn_out", "w_out", "norm_ffn_g",
        "w_ffn_in", "ffn_conv_w", "ffn_conv_b", "w_ffn_down", "norm_final_g"]


def kernel(**inputs):
    import concourse.bacc as bacc
    from concourse.bass_utils import run_bass_kernel_spmd

    nc = bacc.Bacc("TRN2", target_bir_lowering=False, num_devices=1)
    arrays = {f"in_{name}": np.ascontiguousarray(inputs[name]) for name in _INS}
    half = np.exp(np.float32(-math.log(10000.0)) * np.arange(HD // 2, dtype=np.float32) * np.float32(2.0 / HD))
    cols = np.stack([np.tile(half, 2), np.repeat([1.0, -1.0], HD // 2), np.full(HD, math.pi / 2)], axis=1)
    arrays["in_rope_cols"] = np.ascontiguousarray(cols.astype(np.float32))
    args = [nc.dram_tensor(n, a.shape, mybir.dt.from_np(a.dtype), kind="ExternalInput").ap()
            for n, a in arrays.items()]
    out = nc.dram_tensor("out", (1, S, D), F32, kind="ExternalOutput").ap()
    layer(nc, *args, out)
    result = run_bass_kernel_spmd(nc, [arrays], core_ids=[0])
    return result.results[0]["out"]
```
